# Optimizing a Trainium2 kernel written in Bass

```python
import jax
import jax.numpy as jnp
from jax import lax
import numpy as np
import jax, jax.numpy as jnp

D_MODEL = 1024
BATCH = 1
SEQ = 512
DEPTH = 1

GRID_W = 64
CTX_LEN = 256
N_HEADS_NA = 8
HEAD_DIM_NA = 64
WIN_H = 8
WIN_W = 16
NA_QCOLS = 16
NA_KCOLS = 32
N_HEADS_MLA = 8
MLA_Q_RANK = 768
MLA_KV_RANK = 256
MLA_NOPE_DIM = 64
MLA_ROPE_DIM = 32
MLA_V_DIM = 64
D_FF = 2816
ROPE_BASE = 10000.0
RMS_EPS = 1e-6
ATTN_QBLOCK = 128
N_MOD = 9
HALF_STEP = 0.5
NA_WIDTH = N_HEADS_NA * HEAD_DIM_NA
MLA_QK_DIM = MLA_NOPE_DIM + MLA_ROPE_DIM
IN_SPLITS = (NA_WIDTH, 2 * NA_WIDTH, 3 * NA_WIDTH, 3 * NA_WIDTH + MLA_Q_RANK,
             3 * NA_WIDTH + MLA_Q_RANK + MLA_KV_RANK,
             3 * NA_WIDTH + MLA_Q_RANK + MLA_KV_RANK + MLA_ROPE_DIM)
IN_COLS = IN_SPLITS[-1] + 2 * D_MODEL


def _rmsnorm(x, g):
    x32 = x.astype(jnp.float32)
    y = x32 * lax.rsqrt(jnp.mean(x32 * x32, axis=-1, keepdims=True) + RMS_EPS)
    return y.astype(x.dtype) * g

def _modnorm(x, g_pre, shift, scale):
    return _rmsnorm(x, g_pre) * (1 + scale) + shift

def _residual(x, y, g_post, gate, weight):
    return x + weight * gate * _rmsnorm(y, g_post)

def _swiglu(h, w1, w3, w2):
    return (jax.nn.silu(h @ w1) * (h @ w3)) @ w2

def _axial_angles(n_tokens):
    half = MLA_ROPE_DIM // 4
    freqs = ROPE_BASE ** (-jnp.arange(half, dtype=jnp.float32) / half)
    t = jnp.arange(n_tokens)
    rows = (t // GRID_W).astype(jnp.float32)
    cols = (t % GRID_W).astype(jnp.float32)
    return rows[:, None] * freqs, cols[:, None] * freqs

def _rope_axis(x, ang):
    half = x.shape[-1] // 2
    cos = jnp.cos(ang)[None, :, None, :].astype(x.dtype)
    sin = jnp.sin(ang)[None, :, None, :].astype(x.dtype)
    x1, x2 = x[..., :half], x[..., half:]
    return jnp.concatenate([x1 * cos - x2 * sin, x2 * cos + x1 * sin], axis=-1)

def _axial_rope(x, ang_r, ang_c):
    a = MLA_ROPE_DIM // 2
    return jnp.concatenate([_rope_axis(x[..., :a], ang_r), _rope_axis(x[..., a:], ang_c)], axis=-1)

def _project(h, w_in, b_gate, g_q, g_kv, w_uq, w_ukv):
    B, T, _ = h.shape
    qa, ka, va, cq, ckv, kr, gates = jnp.split(h @ w_in, IN_SPLITS, axis=-1)
    heads = lambda t, n: t.reshape(B, T, n, -1)
    q = heads(_rmsnorm(cq, g_q) @ w_uq, N_HEADS_MLA)
    kv = heads(_rmsnorm(ckv, g_kv) @ w_ukv, N_HEADS_MLA)
    g = jax.nn.sigmoid(gates + b_gate)
    return (heads(qa, N_HEADS_NA), heads(ka, N_HEADS_NA), heads(va, N_HEADS_NA),
            q[..., :MLA_NOPE_DIM], q[..., MLA_NOPE_DIM:],
            kv[..., :MLA_NOPE_DIM], kr[:, :, None, :], kv[..., MLA_NOPE_DIM:],
            g[..., :D_MODEL], g[..., D_MODEL:])

def _mla_q(q_nope, q_rope):
    return jnp.concatenate([q_nope, q_rope], axis=-1)

def _mla_k(k_nope, k_rope):
    k_rope = jnp.broadcast_to(k_rope, k_nope.shape[:-1] + (k_rope.shape[-1],))
    return jnp.concatenate([k_nope, k_rope], axis=-1)

def _attend(q, k, v):
    s = jnp.einsum('bqhd,bkhd->bhqk', q * q.shape[-1] ** -0.5, k).astype(jnp.float32)
    p = jax.nn.softmax(s, axis=-1).astype(v.dtype)
    return jnp.einsum('bhqk,bkhd->bqhd', p, v)

def _blocked_attention(q, k, v):
    B, S, H, dq = q.shape
    qb = q.reshape(B, S // ATTN_QBLOCK, ATTN_QBLOCK, H, dq).swapaxes(0, 1)
    out = lax.map(lambda qq: _attend(qq, k, v), qb)
    return out.swapaxes(0, 1).reshape(B, S, H, v.shape[-1])

def _na_column_tables():
    n_blk = GRID_W // NA_QCOLS
    j = np.arange(n_blk)
    k_start = np.clip(j * NA_QCOLS - WIN_W // 2, 0, GRID_W - NA_KCOLS)
    key_col = k_start[:, None] + np.arange(NA_KCOLS)
    q_col = j[:, None] * NA_QCOLS + np.arange(NA_QCOLS)
    w_start = np.clip(q_col - WIN_W // 2, 0, GRID_W - WIN_W)
    kc = key_col[:, None, :]
    valid = (kc >= w_start[..., None]) & (kc < w_start[..., None] + WIN_W)
    off = np.clip(kc - q_col[..., None], -(WIN_W - 1), WIN_W - 1) + (WIN_W - 1)
    return jnp.asarray(key_col, jnp.int32), jnp.asarray(valid), jnp.asarray(off, jnp.int32)

def _neighbourhood_attention(q, k, v, k_ctx, v_ctx, rpb, n_rows):
    B, S, H, d = q.shape
    kh = min(WIN_H, n_rows)
    n_blk = GRID_W // NA_QCOLS
    n_loc = kh * NA_KCOLS
    key_col, valid, col_off = _na_column_tables()
    grid = lambda t: t.reshape(B, n_rows, GRID_W, H, t.shape[-1])
    qg, kg, vg = grid(q * d ** -0.5), grid(k), grid(v)
    neg = jnp.finfo(jnp.float32).min

    def row(r):
        rs = jnp.clip(r - kh // 2, 0, n_rows - kh)
        q_r = lax.dynamic_index_in_dim(qg, r, axis=1, keepdims=False).reshape(B, n_blk, NA_QCOLS, H, d)
        k_b = jnp.moveaxis(lax.dynamic_slice_in_dim(kg, rs, kh, axis=1)[:, :, key_col], 2, 1)
        v_b = jnp.moveaxis(lax.dynamic_slice_in_dim(vg, rs, kh, axis=1)[:, :, key_col], 2, 1)
        row_off = rs + jnp.arange(kh) - r + (WIN_H - 1)
        bias = rpb[:, row_off[None, None, :, None], col_off[:, :, None, :]]
        s_loc = jnp.einsum('bjqhd,bjakhd->bhjqak', q_r, k_b).astype(jnp.float32) + bias.astype(jnp.float32)
        s_loc = jnp.where(valid[:, :, None, :], s_loc, neg).reshape(B, H, n_blk, NA_QCOLS, n_loc)
        s_ctx = jnp.einsum('bjqhd,bkhd->bhjqk', q_r, k_ctx).astype(jnp.float32)
        p = jax.nn.softmax(jnp.concatenate([s_loc, s_ctx], axis=-1), axis=-1).astype(v.dtype)
        p_loc = p[..., :n_loc].reshape(B, H, n_blk, NA_QCOLS, kh, NA_KCOLS)
        o = (jnp.einsum('bhjqak,bjakhd->bjqhd', p_loc, v_b)
             + jnp.einsum('bhjqk,bkhd->bjqhd', p[..., n_loc:], v_ctx))
        return o.reshape(B, GRID_W, H, v.shape[-1])

    out = lax.map(row, jnp.arange(n_rows))
    return jnp.moveaxis(out, 0, 1).reshape(B, S, H, v.shape[-1])

def _merge(o_na, o_mla, g_na, g_mla, w_o_na, w_o_mla, w_out):
    B, T = o_na.shape[:2]
    y = g_na * (o_na.reshape(B, T, -1) @ w_o_na) + g_mla * (o_mla.reshape(B, T, -1) @ w_o_mla)
    return y @ w_out

def first_inputs(seed: int = 0) -> dict:
    key = jax.random.key(seed)
    ks = jax.random.split(key, 24)
    nrm = lambda k, shape, s: jax.random.normal(k, shape, jnp.float32) * s
    D = D_MODEL
    return {
        'x': nrm(ks[0], (BATCH, SEQ, D), 1.0),
        'c': nrm(ks[1], (BATCH, D), 1.0),
        'ctx': nrm(ks[2], (BATCH, CTX_LEN, D), 1.0),
        'c_ctx': nrm(ks[3], (D,), 1.0),
        'w_ada': nrm(ks[4], (DEPTH, D, N_MOD * D), 0.5 * D ** -0.5),
        'b_ada': nrm(ks[5], (DEPTH, N_MOD * D), 0.02),
        'norm_g': 1.0 + nrm(ks[6], (DEPTH, 6, D), 0.02),
        'ffn1_w1': nrm(ks[7], (DEPTH, D, D_FF), D ** -0.5),
        'ffn1_w3': nrm(ks[8], (DEPTH, D, D_FF), D ** -0.5),
        'ffn1_w2': nrm(ks[9], (DEPTH, D_FF, D), D_FF ** -0.5),
        'w_in': nrm(ks[10], (DEPTH, D, IN_COLS), D ** -0.5),
        'b_gate': nrm(ks[11], (DEPTH, 2 * D), 0.1),
        'g_q_lora': 1.0 + nrm(ks[12], (DEPTH, MLA_Q_RANK), 0.02),
        'g_kv_lora': 1.0 + nrm(ks[13], (DEPTH, MLA_KV_RANK), 0.02),
        'w_uq': nrm(ks[14], (DEPTH, MLA_Q_RANK, N_HEADS_MLA * MLA_QK_DIM), MLA_Q_RANK ** -0.5),
        'w_ukv': nrm(ks[15], (DEPTH, MLA_KV_RANK, N_HEADS_MLA * (MLA_NOPE_DIM + MLA_V_DIM)), MLA_KV_RANK ** -0.5),
        'rpb': nrm(ks[16], (DEPTH, N_HEADS_NA, 2 * WIN_H - 1, 2 * WIN_W - 1), 0.1),
        'w_o_na': nrm(ks[17], (DEPTH, NA_WIDTH, D), NA_WIDTH ** -0.5),
        'w_o_mla': nrm(ks[18], (DEPTH, N_HEADS_MLA * MLA_V_DIM, D), (N_HEADS_MLA * MLA_V_DIM) ** -0.5),
        'w_out': nrm(ks[19], (DEPTH, D, D), D ** -0.5),
        'ffn2_w1': nrm(ks[20], (DEPTH, D, D_FF), D ** -0.5),
        'ffn2_w3': nrm(ks[21], (DEPTH, D, D_FF), D ** -0.5),
        'ffn2_w2': nrm(ks[22], (DEPTH, D_FF, D), D_FF ** -0.5),
    }

def first_block(x, c, ctx, c_ctx, w_ada, b_ada, norm_g, ffn1_w1, ffn1_w3, ffn1_w2, w_in, b_gate,
              g_q_lora, g_kv_lora, w_uq, w_ukv, rpb, w_o_na, w_o_mla, w_out, ffn2_w1, ffn2_w3, ffn2_w2):
    n_lat = x.shape[1]
    n_rows = n_lat // GRID_W
    ang_r, ang_c = _axial_angles(n_lat)
    h_ctx = ctx
    for l in range(DEPTH):
        last = l == DEPTH - 1
        m = jnp.split((jax.nn.silu(c) @ w_ada[l] + b_ada[l])[:, None, :], N_MOD, axis=-1)
        mc = jnp.split(jax.nn.silu(c_ctx) @ w_ada[l] + b_ada[l], N_MOD, axis=-1)
        g = norm_g[l]
        x = _residual(x, _swiglu(_modnorm(x, g[0], m[0], m[1]), ffn1_w1[l], ffn1_w3[l], ffn1_w2[l]),
                      g[1], m[2], HALF_STEP)
        h_ctx = _residual(h_ctx, _swiglu(_modnorm(h_ctx, g[0], mc[0], mc[1]), ffn1_w1[l], ffn1_w3[l], ffn1_w2[l]),
                          g[1], mc[2], HALF_STEP)
        pw = (w_in[l], b_gate[l], g_q_lora[l], g_kv_lora[l], w_uq[l], w_ukv[l])
        qa, ka, va, qn, qr, kn, kr, vb, ga, gb = _project(_modnorm(x, g[2], m[3], m[4]), *pw)
        cqa, cka, cva, cqn, cqr, ckn, ckr, cvb, cga, cgb = _project(_modnorm(h_ctx, g[2], mc[3], mc[4]), *pw)
        o_na = _neighbourhood_attention(qa, ka, va, cka, cva, rpb[l], n_rows)
        k_ctx_mla = _mla_k(ckn, ckr)
        q_mla = _mla_q(qn, _axial_rope(qr, ang_r, ang_c))
        k_mla = jnp.concatenate([k_ctx_mla, _mla_k(kn, _axial_rope(kr, ang_r, ang_c))], axis=1)
        v_mla = jnp.concatenate([cvb, vb], axis=1)
        o_mla = _blocked_attention(q_mla, k_mla, v_mla)
        y = _merge(o_na, o_mla, ga, gb, w_o_na[l], w_o_mla[l], w_out[l])
        x = _residual(x, y, g[3], m[5], 1.0)
        if not last:
            yc = _merge(_attend(cqa, cka, cva), _attend(_mla_q(cqn, cqr), k_ctx_mla, cvb),
                        cga, cgb, w_o_na[l], w_o_mla[l], w_out[l])
            h_ctx = _residual(h_ctx, yc, g[3], mc[5], 1.0)
            h_ctx = _residual(h_ctx, _swiglu(_modnorm(h_ctx, g[4], mc[6], mc[7]), ffn2_w1[l], ffn2_w3[l], ffn2_w2[l]),
                              g[5], mc[8], HALF_STEP)
        x = _residual(x, _swiglu(_modnorm(x, g[4], m[6], m[7]), ffn2_w1[l], ffn2_w3[l], ffn2_w2[l]),
                      g[5], m[8], HALF_STEP)
    return x


PLE_DIM = 256
ML_HEADS = 4
ML_DQK = 128
ML_DV = 256
ML_CONV = 4
ML_CHUNK = 64
SW_Q_HEADS = 16
SW_KV_HEADS = 4
SW_HEAD_DIM = 64
SW_WINDOW = 128
D_FF_2 = 4 * D_MODEL
EPS = 1e-6

ML_QK_W = ML_HEADS * ML_DQK
ML_V_W = ML_HEADS * ML_DV
SW_Q_W = SW_Q_HEADS * SW_HEAD_DIM
SW_KV_W = SW_KV_HEADS * SW_HEAD_DIM
SPLIT_SIZES = (2 * ML_QK_W, ML_V_W, ML_V_W, 2 * ML_HEADS, SW_Q_W, SW_KV_W, SW_KV_W, D_MODEL, D_MODEL)
N_IN = sum(SPLIT_SIZES)


def rmsnorm(x, g):
    xf = x.astype(jnp.float32)
    xf = xf * lax.rsqrt(jnp.mean(xf * xf, axis=-1, keepdims=True) + EPS)
    return xf.astype(x.dtype) * g.astype(x.dtype)

def causal_depthwise_conv(x, w):
    c = x.shape[-1]
    return lax.conv_general_dilated(
        x, w.astype(x.dtype)[:, None, :], window_strides=(1,), padding=((ML_CONV - 1, 0),),
        dimension_numbers=("NWC", "WIO", "NWC"), feature_group_count=c)

def mlstm_chunkwise(q, k, v, ig, lf):
    B, S = q.shape[:2]
    L = ML_CHUNK
    nc = S // L

    def to_chunks(t):
        t = t.astype(jnp.float32).reshape((B, nc, L) + t.shape[2:])
        return jnp.moveaxis(jnp.moveaxis(t, 1, 0), 3, 2)

    xs = (to_chunks(q), to_chunks(k), to_chunks(v), to_chunks(ig), to_chunks(lf))
    causal = jnp.tril(jnp.ones((L, L), dtype=bool))

    def step(carry, chunk):
        C, n, m = carry
        qc, kc, vc, ic, fc = chunk
        b = jnp.cumsum(fc, axis=-1)
        log_d = jnp.where(causal, b[..., :, None] - b[..., None, :] + ic[..., None, :], -jnp.inf)
        inter = b + m[..., None]
        m_t = jnp.maximum(inter, jnp.max(log_d, axis=-1))
        scores = jnp.einsum("bhtk,bhsk->bhts", qc, kc) * jnp.exp(log_d - m_t[..., None])
        w_inter = jnp.exp(inter - m_t)
        num = (w_inter[..., None] * jnp.einsum("bhvk,bhtk->bhtv", C, qc)
               + jnp.einsum("bhts,bhsv->bhtv", scores, vc))
        den = w_inter * jnp.einsum("bhk,bhtk->bht", n, qc) + jnp.sum(scores, axis=-1)
        h = num / jnp.maximum(jnp.abs(den), jnp.exp(-m_t))[..., None]
        b_last = b[..., -1]
        log_w = b_last[..., None] - b + ic
        m_new = jnp.maximum(b_last + m, jnp.max(log_w, axis=-1))
        w = jnp.exp(log_w - m_new[..., None])
        decay = jnp.exp(b_last + m - m_new)
        C_new = decay[..., None, None] * C + jnp.einsum("bhs,bhsv,bhsk->bhvk", w, vc, kc)
        n_new = decay[..., None] * n + jnp.einsum("bhs,bhsk->bhk", w, kc)
        return (C_new, n_new, m_new), h

    H, dk, dv = q.shape[2], q.shape[3], v.shape[3]
    init = (jnp.zeros((B, H, dv, dk), jnp.float32), jnp.zeros((B, H, dk), jnp.float32),
            jnp.zeros((B, H), jnp.float32))
    _, h = lax.scan(step, init, xs)
    h = jnp.moveaxis(jnp.moveaxis(h, 2, 3), 0, 1)
    return h.reshape(B, S, H, dv)

def swa_with_sinks(q, k, v, sinks):
    B, S = q.shape[:2]
    W = SW_WINDOW
    nb = S // W
    G = SW_Q_HEADS // SW_KV_HEADS
    qb = q.reshape(B, nb, W, SW_KV_HEADS, G, SW_HEAD_DIM)

    def band(t):
        tb = t.reshape(B, nb, W, SW_KV_HEADS, SW_HEAD_DIM)
        prev = jnp.pad(tb, ((0, 0), (1, 0), (0, 0), (0, 0), (0, 0)))[:, :-1]
        return jnp.concatenate([prev, tb], axis=2)

    kb, vb = band(k), band(v)
    logits = jnp.einsum("bnqhgd,bnkhd->bnhgqk", qb, kb).astype(jnp.float32) * (SW_HEAD_DIM ** -0.5)
    qi = jnp.arange(W)[:, None]
    ki = jnp.arange(2 * W)[None, :]
    diff = qi + W - ki
    band_mask = (diff >= 0) & (diff < W)
    valid = band_mask[None] & ((jnp.arange(nb)[:, None, None] > 0) | (ki >= W)[None])
    logits = jnp.where(valid[None, :, None, None], logits, -jnp.inf)
    sink = sinks.astype(jnp.float32).reshape(SW_KV_HEADS, G)[None, None, :, :, None, None]
    m = jnp.maximum(jnp.max(logits, axis=-1, keepdims=True), sink)
    pexp = jnp.exp(logits - m)
    probs = pexp / (jnp.sum(pexp, axis=-1, keepdims=True) + jnp.exp(sink - m))
    out = jnp.einsum("bnhgqk,bnkhd->bnqhgd", probs.astype(v.dtype), vb)
    return out.reshape(B, S, SW_Q_W)

def second_inputs(seed: int = 0) -> dict:
    key = jax.random.key(seed)
    ks = jax.random.split(key, 20)
    f32 = jnp.float32
    nrm = lambda k, shape, s: jax.random.normal(k, shape, f32) * s
    gain = lambda k, shape: 1.0 + 0.05 * jax.random.normal(k, shape, f32)
    b_if = jnp.concatenate([
        0.1 * jax.random.normal(ks[3], (DEPTH, ML_HEADS), f32),
        3.0 + 0.5 * jax.random.normal(ks[4], (DEPTH, ML_HEADS), f32),
    ], axis=-1)
    return {
        "x": jax.random.normal(ks[0], (BATCH, SEQ, D_MODEL), f32),
        "p": jax.random.normal(ks[1], (DEPTH, BATCH, SEQ, PLE_DIM), f32),
        "norm_mix_g": gain(ks[2], (DEPTH, D_MODEL)),
        "w_in": nrm(ks[5], (DEPTH, D_MODEL, N_IN), D_MODEL ** -0.5),
        "conv_qk": nrm(ks[6], (DEPTH, ML_CONV, 2 * ML_QK_W), ML_CONV ** -0.5),
        "b_if": b_if,
        "mlstm_norm_g": gain(ks[7], (DEPTH, ML_V_W)),
        "sinks": nrm(ks[8], (DEPTH, SW_Q_HEADS), 0.5),
        "w_branch_a": nrm(ks[9], (DEPTH, ML_V_W, D_MODEL), ML_V_W ** -0.5),
        "w_branch_b": nrm(ks[10], (DEPTH, SW_Q_W, D_MODEL), SW_Q_W ** -0.5),
        "w_out": nrm(ks[11], (DEPTH, D_MODEL, D_MODEL), D_MODEL ** -0.5),
        "norm_mlp_g": gain(ks[12], (DEPTH, D_MODEL)),
        "w_up": nrm(ks[13], (DEPTH, D_MODEL, D_FF_2), D_MODEL ** -0.5),
        "w_down": nrm(ks[14], (DEPTH, D_FF_2, D_MODEL), D_FF_2 ** -0.5),
        "norm_ple_g": gain(ks[15], (DEPTH, D_MODEL)),
        "w_ple_gate": nrm(ks[16], (DEPTH, D_MODEL, D_MODEL), D_MODEL ** -0.5),
        "w_ple_proj": nrm(ks[17], (DEPTH, PLE_DIM, D_MODEL), PLE_DIM ** -0.5),
        "final_norm_g": gain(ks[18], (D_MODEL,)),
    }

def second_block(x, p, norm_mix_g, w_in, conv_qk, b_if, mlstm_norm_g, sinks, w_branch_a, w_branch_b,
              w_out, norm_mlp_g, w_up, w_down, norm_ple_g, w_ple_gate, w_ple_proj, final_norm_g):
    B, S, _ = x.shape
    split_idx = [int(v) for v in np.cumsum(SPLIT_SIZES)[:-1]]
    for i in range(DEPTH):
        h = rmsnorm(x, norm_mix_g[i])
        proj = h @ w_in[i]
        qk_ml, v_ml, o_ml, if_pre, q_sw, k_sw, v_sw, g_a, g_b = jnp.split(proj, split_idx, axis=-1)

        qk_ml = jax.nn.silu(causal_depthwise_conv(qk_ml, conv_qk[i]))
        q_ml, k_ml = jnp.split(qk_ml, 2, axis=-1)
        q_ml = q_ml.reshape(B, S, ML_HEADS, ML_DQK) * (ML_DQK ** -0.5)
        k_ml = k_ml.reshape(B, S, ML_HEADS, ML_DQK)
        gates = (if_pre + b_if[i].astype(if_pre.dtype)).astype(jnp.float32)
        ig = gates[..., :ML_HEADS]
        lf = jax.nn.log_sigmoid(gates[..., ML_HEADS:])
        h_ml = mlstm_chunkwise(q_ml, k_ml, v_ml.reshape(B, S, ML_HEADS, ML_DV), ig, lf)
        h_ml = h_ml * lax.rsqrt(jnp.mean(h_ml * h_ml, axis=-1, keepdims=True) + EPS)
        h_ml = h_ml.reshape(B, S, ML_V_W).astype(x.dtype) * mlstm_norm_g[i].astype(x.dtype)
        y_a = jax.nn.sigmoid(o_ml) * h_ml

        y_b = swa_with_sinks(q_sw.reshape(B, S, SW_Q_HEADS, SW_HEAD_DIM),
                             k_sw.reshape(B, S, SW_KV_HEADS, SW_HEAD_DIM),
                             v_sw.reshape(B, S, SW_KV_HEADS, SW_HEAD_DIM), sinks[i])

        merged = jax.nn.sigmoid(g_a) * (y_a @ w_branch_a[i]) + jax.nn.sigmoid(g_b) * (y_b @ w_branch_b[i])
        x = x + merged @ w_out[i]

        u = rmsnorm(x, norm_mlp_g[i]) @ w_up[i]
        x = x + jnp.square(jax.nn.relu(u)) @ w_down[i]

        gate = jax.nn.sigmoid(rmsnorm(x, norm_ple_g[i]) @ w_ple_gate[i])
        x = x + gate * (p[i].astype(x.dtype) @ w_ple_proj[i])
    return rmsnorm(x, final_norm_g)


def setup_inputs(seed=0):
    out = dict(first_inputs(seed))
    for name, value in second_inputs(seed + 1).items():
        if name != "x":
            out[name + "_2"] = value
    return out


def reference(
    x, c, ctx, c_ctx, w_ada, b_ada, norm_g, ffn1_w1, ffn1_w3, ffn1_w2, w_in, b_gate, g_q_lora,
    g_kv_lora, w_uq, w_ukv, rpb, w_o_na, w_o_mla, w_out, ffn2_w1, ffn2_w3, ffn2_w2, p_2,
    norm_mix_g_2, w_in_2, conv_qk_2, b_if_2, mlstm_norm_g_2, sinks_2, w_branch_a_2,
    w_branch_b_2, w_out_2, norm_mlp_g_2, w_up_2, w_down_2, norm_ple_g_2, w_ple_gate_2,
    w_ple_proj_2, final_norm_g_2,
):
    x = first_block(
        x, c, ctx, c_ctx, w_ada, b_ada, norm_g, ffn1_w1, ffn1_w3, ffn1_w2, w_in, b_gate,
        g_q_lora, g_kv_lora, w_uq, w_ukv, rpb, w_o_na, w_o_mla, w_out, ffn2_w1, ffn2_w3,
        ffn2_w2,
    )
    return second_block(
        x, p_2, norm_mix_g_2, w_in_2, conv_qk_2, b_if_2, mlstm_norm_g_2, sinks_2, w_branch_a_2,
        w_branch_b_2, w_out_2, norm_mlp_g_2, w_up_2, w_down_2, norm_ple_g_2, w_ple_gate_2,
        w_ple_proj_2, final_norm_g_2,
    )


_drawn_inputs = setup_inputs


def setup_inputs(seed=0):
    import zlib

    import numpy as np

    out = dict(_drawn_inputs(seed))
    spreads = {}
    factors = {'norm_g': 4.601,
     'b_gate': 3.954,
     'g_q_lora': 8.0,
     'g_kv_lora': 8.0,
     'rpb': 8.0,
     'mlstm_norm_g_2': 4.099,
     'sinks_2': 36.306,
     'norm_ple_g_2': 35.088}
    for name, (base, spread) in spreads.items():
        noise = np.random.default_rng([zlib.crc32(name.encode()), seed]).standard_normal(out[name].shape)
        drawn = base * np.exp(spread * noise) if base else spread * noise
        out[name] = jnp.asarray(drawn.astype(out[name].dtype))
    for name, factor in factors.items():
        out[name] = (out[name] * factor).astype(out[name].dtype)
    return out
```

```python
from contextlib import ExitStack

import numpy as np

import concourse.bass as bass
from concourse import mybir

F32 = mybir.dt.float32
ALU = mybir.AluOpType
ACT = mybir.ActivationFunctionType
AX = mybir.AxisListType

P = 128
D = 1024
KC = D // P
S = 512
CTX = 256
T = S + CTX
EPS = 1e-6
NEG = -1e30
N_MOD = 9
GRID_W, GRID_H = 64, 8
N_BLK, Q_COLS, K_COLS, WIN_W = 4, 16, 32, 16
K_START = [min(max(j * Q_COLS - WIN_W // 2, 0), GRID_W - K_COLS) for j in range(N_BLK)]
NA_HEADS, NA_D = 8, 64
ML_Q_RANK, ML_KV_RANK, NOPE, ROPE, V_D = 768, 256, 64, 32, 64
QK_D = NOPE + ROPE
QR, KVR = ML_Q_RANK // P, ML_KV_RANK // P
FF = 2816 // P
FF2 = 4 * D // P
RPB_H, RPB_W = 15, 31
BIAS_W = K_COLS + Q_COLS
X_HEADS, X_DK, X_DV = 4, 128, 256
SW_HEADS, SW_KV, SW_D, SW_W = 16, 4, 64, 128

RING = 4
UNIT = 16 * P
UNITS = [
    ("ada_head", 8, UNIT), ("up1_ada", 2 * FF, UNIT), ("down1", 16, 11 * P), ("ada_tail", 6, UNIT),
    ("proj", 10, UNIT), ("kr", 1, KC * QK_D), ("uq", 4, 2 * QR * QK_D), ("ukv_k", 1, NA_HEADS * KVR * NOPE),
    ("ukv_v", 1, KVR * 512), ("merge1", 16, 12 * P), ("out1", 4, UNIT), ("up2", FF, UNIT), ("down2", 16, 11 * P),
    ("qk_m", 4, UNIT), ("v_m", 4, UNIT), ("q_sw", 4, UNIT), ("k_sw", 1, UNIT), ("v_sw", 1, UNIT),
    ("if_m", 1, KC * 36), ("o_m", 4, UNIT), ("merge2", 16, UNIT), ("out2", 4, UNIT), ("up3", 16, UNIT),
    ("down3", 16, UNIT), ("ple", 8, 10 * P),
]
BASE, _n = {}, 0
for _name, _count, _floats in UNITS:
    BASE[_name] = _n
    _n += _count
N_UNITS = _n


def _places(columns):
    at, out = 0, {}
    for name, n in columns:
        out[name] = at
        at += n
    return out, at


PARAM, N_PARAM = _places([("b_ada", 2 * N_MOD * KC), ("norm_g", 2 * 6 * KC), ("b_gate", 2 * KC), ("g_q", QR),
                          ("g_kv", KVR), ("mix_g", KC), ("mlstm_g", KC), ("mlp_g", KC), ("ple_g", KC),
                          ("final_g", KC), ("conv", 4 * KC), ("sinks", SW_HEADS), ("b_if", 2), ("eps", 1)])
CONST, N_CONST = _places([("ident", P), ("ones", P), ("rot", QK_D), ("cos", S), ("sin", S), ("select", 4 * P),
                          ("na_mask", N_BLK * K_COLS), ("sw_mask", 2 * P), ("causal", P)])
LAT = [(0, S, 0)]
BOTH = [(0, S, 0), (S, T, 1)]
NA_S = (0, 1, 6)
SCALE1, SCALE2, SCALE3, GATE1, GATE2, GATE3 = range(6)


def build(nc, xT, cT, params, consts, weights, rpb, pT, out):
    with ExitStack() as ctx:
        def sb(name, n):
            return ctx.enter_context(nc.sbuf_tensor(name, [P, n], F32))

        def sem(name):
            return ctx.enter_context(nc.semaphore(name))

        def view(t, at, a, b):
            return t[:, at:at + a * b].rearrange("p (a b) -> p a b", a=a)

        bank = ctx.enter_context(nc.psum_tensor("banks", [P, 8, 512], F32))
        x_t = sb("residual", KC * T)
        h_t = sb("normed", KC * T)
        big = sb("big", 20736)
        ring = sb("weight_ring", RING * UNIT)
        sq_t = sb("scratch_a", 2 * T)
        tmp_t = sb("scratch_b", 2 * T)
        rs = sb("rstd", T)
        prm = sb("params_sb", N_PARAM)
        cst = sb("consts_sb", N_CONST)
        bias_t = sb("rpb_rows", NA_HEADS * GRID_H * BIAS_W)
        BIAS = bias_t[:, :].rearrange("p (h a w) -> p h a w", h=NA_HEADS, a=GRID_H)
        mods_t = sb("mods", 2 * N_MOD * KC)
        coef_t = sb("coefs", 6 * KC * 2)
        cvec = sb("cvec", KC * 2)
        cs = sb("silu_c", KC * 2)
        stat = sb("stat", 64)
        bm_t = sb("bias_mask", 2 * 256)
        p_sb = sb("p_embed", 2 * S)

        X = view(x_t, 0, KC, T)
        H = view(h_t, 0, KC, T)
        SQ = view(sq_t, 0, 2, T)
        TMP = view(tmp_t, 0, 2, T)
        SQ5 = view(sq_t, 0, 3, S)
        TMP5 = view(tmp_t, 0, 3, S)
        MODS = mods_t[:, :].rearrange("p (m c) -> p m c", c=2)
        COEF = coef_t[:, :].rearrange("p (g k c) -> p g k c", g=6, c=2)
        PE2 = view(p_sb, 0, 2, S)
        CVEC = cvec[:, :].rearrange("p (k c) -> p k c", c=2)
        CS = cs[:, :].rearrange("p (k c) -> p k c", c=2)

        def par(name, i=0, n=1, rows=P):
            return prm[0:rows, PARAM[name] + i:PARAM[name] + i + n]

        def con(name, i, n, rows=P):
            return cst[0:rows, CONST[name] + i:CONST[name] + i + n]

        ident, ones = con("ident", 0, P), con("ones", 0, P)
        eps = par("eps")

        HID = view(big, 0, FF, T)
        QA = view(big, 0, 4, S)
        KA = view(big, 2048, 4, T)
        VA = view(big, 5120, 4, N_BLK * 256 + CTX)
        CQ = view(big, 10240, QR, S)
        CKV = view(big, 13312, KVR, T)
        KR = big[:, 14848:14848 + T]
        VN = view(big, 15616, 10, 512)
        KM = view(big, 2048, NA_HEADS, T)
        OM = view(big, 8192, 4, S)
        QM = view(big, 15616, NA_HEADS, S)
        VM = view(big, 10240, 6, 512)
        PM = view(big, 13312, 3, T)
        MR1 = view(big, 2048, KC, S)
        HID2 = view(big, 0, FF2, S)
        QK = view(big, 0, 8, S)
        VX = view(big, 4096, 4, 1024)
        QS = view(big, 8192, 8, S)
        KS = view(big, 12288, SW_KV, S)
        VS = view(big, 14336, 4, 256)
        YA = view(big, 15360, 8, S)
        MR2 = view(big, 0, KC, S)
        ROWS = view(big, 12288, 6, S)
        ACOL = big[:, 19456:19456 + 16].rearrange("p (c h) -> p c h", c=4)

        landed = [sem(f"weights_landed_{i}") for i in range(RING)]
        unit_begun = sem("unit_begun")
        inputs_landed, rpb_landed, stored = sem("inputs_landed"), sem("rpb_landed"), sem("output_stored")
        N_LOADS = 6
        dve_c = sem("dve_chain")

        def stages(count, name, *signals):
            shared = {s: sem(f"{name}_{s}") for s in signals}
            return [dict(shared, base=i * KC, turn=i) for i in range(count)]

        def st(name, *signals):
            return stages(1, name, *signals)[0]

        ada = st("ada", "silu", "done", "got", "tail", "tail_got")
        up1, up2, up3 = (st(f"up{i}", "done", "act", "free") for i in (1, 2, 3))
        down1, out1, down2 = stages(3, "sublayer", "done", "free", "sq", "sq_used")
        out2, down3 = stages(2, "add", "done")
        n0 = st("norm_0", "sq", "sq_used", "root", "scaled", "ready")
        na, nb = (st(f"norm_{n}", "y_root", "xnew", "sq", "sq_used", "root", "scaled", "ready") for n in ("a", "b"))
        nmix = st("norm_mix", "y_root", "xnew", "sq", "sq_used", "root", "ready")
        nmlp, nple, nfin = stages(3, "norm_late", "xnew", "sq", "sq_used", "root", "ready")
        proj = st("proj", "done", "act", "dve")
        vt = st("vt", "done", "act", "dve")
        ana = st("att_na", "s", "bias", "biased", "max", "exp", "norm", "t", "tc", "pv", "oc")
        amla = st("att_mla", "s", "max", "exp", "norm", "t", "tc", "pv", "oc")
        asw = st("att_sw", "s", "biased", "max", "exp", "norm", "t", "tc", "pv", "oc")
        lora = st("lora", "sq", "sq_used", "root", "normed")
        gen = st("mla_gen", "kr", "kr_roped", "q", "qc", "rot", "q_roped", "k", "kc", "v", "vc")
        mrg1, mrg2 = stages(2, "merge", "done", "gate", "free")
        ple = st("ple", "done", "gate", "free")
        conv = st("conv", "raw", "mixed", "ready")
        prj2 = st("proj2", "done", "act", "dve")
        gate = st("gates", "pre", "exp", "lf", "soft", "rows", "cols", "ready")
        ml = st("mlstm", "bcast", "minus_m", "diag", "e", "s", "w", "used", "acc", "floor", "num", "sq", "ssq", "root", "head")
        og = st("ogate", "done", "act", "free")

        block = ctx.enter_context(nc.Block())

        def grid_cols(rows, first):
            return rows.rearrange("p (r w) -> p r w", w=GRID_W)[:, :, first:first + K_COLS]

        def q_blocks(b):
            dst = QA[:, b, :].rearrange("p (j r c) -> p r j c", j=N_BLK, r=GRID_H)
            return dst, bank[:, 2 * (b % 3), :].rearrange("p (r j c) -> p r j c", r=GRID_H, j=N_BLK)

        def v_blocks(b):
            s = b % 3
            pairs = [(VA[:, b - 8, j * 256:(j + 1) * 256].rearrange("p (r w) -> p r w", w=K_COLS),
                      grid_cols(bank[:, 2 * s, :], K_START[j])) for j in range(N_BLK)]
            return pairs + [(VA[:, b - 8, N_BLK * 256:], bank[:, 2 * s + 1, 0:CTX])]

        def slot(n, at=0, k=UNIT):
            base = (n % RING) * UNIT + at
            return ring[:, base:base + k]

        def rounds(eng, lo, hi, body):
            with eng.Fori(lo, hi) as i:
                body(i)

        @block.sync
        def _(sp):
            def load(n, i, floats):
                if n + (0 if isinstance(i, int) else RING) >= RING:
                    sp.wait_ge(unit_begun, i * RING + (n - RING + 2))
                src = weights[n + RING * i] if isinstance(i, int) else \
                    weights[bass.ds(i * RING + n, 1)].rearrange("o p f -> p (o f)")
                sp.dma_start(slot(n, 0, floats), src[:, 0:floats]).then_inc(landed[n % RING], 16)

            for name, count, floats in UNITS:
                n, whole = BASE[name], 0
                if n >= RING and count // RING >= 2:
                    whole = count // RING

                    def body(i):
                        for j in range(RING):
                            load(n + j, i, floats)
                    rounds(sp, 0, whole, body)
                for j in range(whole * RING, count):
                    load(n + j, 0, floats)
            sp.wait_ge(nfin["ready"], 3 * KC)
            sp.dma_start(out.rearrange("(k p) t -> p k t", p=P), H[:, :, 0:S]).then_inc(stored, 16)
            sp.wait_ge(stored, 16)

        @block.tensor
        def _(pe):
            def begin(n, i=0):
                pe.wait_ge(landed[n % RING], i * 16 + 16 * (n // RING + 1))

            def mm(o, w, r, start, stop, first=False):
                ins = nc.tensor.matmul(o, w, r, start=start, stop=stop)
                if first:
                    ins.then_inc(unit_begun, 1)
                return ins

            def sum_squares(g, k, parts, banks, count=KC):
                pe.wait_ge(g["sq"], g["base"] + k + 1)
                for (a, b, _), n in zip(parts, banks):
                    last = nc.tensor.matmul(bank[:, n, 0:b - a], ones, SQ[:, k % 2, a:b],
                                            start=(k == 0), stop=(k == count - 1))
                return last

            def norm_sums(g, parts):
                for k in range(KC):
                    sum_squares(g, k, parts, (6, 5)).then_inc(g["sq_used"], 1)

            def ada_unit(n, i, b, signal):
                begin(n, i)
                for q in range(2):
                    for k in range(KC):
                        last = mm(bank[:, b, 2 * q:2 * q + 2], slot(n, (q * KC + k) * P, P), CS[:, k, :],
                                  k == 0, k == KC - 1, q == 0 and k == 0)
                last.then_inc(signal, 1)

            def swiglu_up(g, n, i, f, s, parts, ready, first):
                begin(n, i)
                for w in range(2):
                    for k in range(KC):
                        if first and w == 0:
                            pe.wait_ge(ready, len(parts) * (k + 1))
                        for a, b, c in parts:
                            o = bank[:, 3 * s + w, 0:S] if c == 0 else bank[:, 3 * s + 2, w * CTX:(w + 1) * CTX]
                            last = mm(o, slot(n, (w * KC + k) * P, P), H[:, k, a:b], k == 0, k == KC - 1,
                                      w == 0 and k == 0 and c == 0)
                last.then_inc(g["done"], 1)

            def out_chunks(g, free, n, i, o0, tiles, rhs, parts, per_unit, sums=None, peel=False):
                unit = -1
                for j in range(2):
                    if not (peel):
                        pe.wait_ge(free, o0 + (g["base"] + j - 1))
                    for t in range(tiles):
                        at = j * tiles + t
                        new = at // per_unit != unit
                        unit = at // per_unit
                        if new:
                            begin(n + unit, i)
                        for a, b, c in parts:
                            last = mm(bank[:, 2 * j + c, 0:b - a], slot(n + unit, (at % per_unit) * P, P),
                                      rhs[:, t, a:b], t == 0, t == tiles - 1, new and c == 0)
                    last.then_inc(g["done"], 1)
                    if sums and not (peel and j == 0):
                        sg, banks = sums
                        pe.wait_ge(sg["sq"], o0 + (sg["base"] + j))
                        for (a, b, _), q in zip(parts, banks):
                            last = nc.tensor.matmul(bank[:, q, 0:b - a], ones, SQ[:, 1 - j, a:b],
                                                    start=(peel and j == 1), stop=False)
                        last.then_inc(sg["sq_used"], 1)

            def out_projection(g, free, name, tiles, rhs, parts, per_unit, sums):
                units = 2 * tiles // per_unit
                out_chunks(g, free, BASE[name], 0, 0, tiles, rhs, parts, per_unit, sums, peel=True)
                if units == RING:
                    rounds(pe, 1, KC // 2, lambda i: out_chunks(g, free, BASE[name], i, 2 * i, tiles, rhs, parts,
                                                                per_unit, sums))
                else:
                    for i in range(1, KC // 2):
                        out_chunks(g, free, BASE[name] + units * i, 0, 2 * i, tiles, rhs, parts, per_unit, sums)
                sg, banks = sums
                sum_squares(sg, KC - 1, parts, banks).then_inc(sg["sq_used"], 1)

            def merged(g, name, per_branch, branch_a, branch_b):
                for o in range(KC):
                    s = o % 2
                    if o >= 2:
                        pe.wait_ge(g["free"], g["base"] + o - 1)
                    for q, rows in ((0, branch_a), (1, branch_b)):
                        n = BASE[name] + 2 * o + q
                        begin(n)
                        for k in range(KC):
                            mm(bank[:, 4 * s + q, :], slot(n, k * P, P), H[:, k, 0:S], k == 0, k == KC - 1, k == 0)
                        for k in range(per_branch):
                            last = mm(bank[:, 4 * s + 2 + q, :], slot(n, (KC + k) * P, P), rows[:, k, :],
                                      k == 0, k == per_branch - 1)
                    last.then_inc(g["done"], 1)

            def attention(g, units, exps, scores, pieces, values, s_sets, t_banks, o_banks, per_out):
                turned = 0
                upto = [0]
                for u in range(units):
                    upto.append(upto[-1] + len(pieces(u)))
                for i in range(units + 3):
                    if i < units:
                        if i >= s_sets:
                            pe.wait_ge(g["exp"], exps * (i - s_sets + 1))
                        scores(i).then_inc(g["s"], 1)
                    if 2 <= i < units + 2:
                        u = i - 2
                        pe.wait_ge(g["norm"], u + 1)
                        for piece in pieces(u):
                            if turned >= len(t_banks):
                                pe.wait_ge(g["tc"], turned - len(t_banks) + 1)
                            for c, source in enumerate(piece):
                                last = nc.tensor.transpose(
                                    bank[:, t_banks[turned % len(t_banks)], c * P:(c + 1) * P], source, ident)
                            last.then_inc(g["t"], 1)
                            turned += 1
                    if i >= 3:
                        u = i - 3
                        pe.wait_ge(g["tc"], upto[u + 1])
                        if u % per_out == 0 and u // per_out >= o_banks:
                            pe.wait_ge(g["oc"], u // per_out - o_banks + 1)
                        values(u).then_inc(g["pv"], 1)

            pe.wait_ge(inputs_landed, 16 * N_LOADS)
            pe.wait_ge(ada["silu"], 1)
            for u in range(8):
                if u >= 2:
                    pe.wait_ge(ada["got"], u - 1)
                ada_unit(BASE["ada_head"] + u, 0, u % 2, ada["done"])
                if u == 3:
                    norm_sums(n0, BOTH)
            pe.wait_ge(ada["got"], 8)

            def up1_round(i, first=False):
                for j in range(2):
                    n = BASE["up1_ada"] + 2 * j
                    if not first:
                        pe.wait_ge(up1["free"], 2 * i + (j - 1))
                    swiglu_up(up1, n, i, 2 * i + j, j, BOTH, n0["ready"], first and j == 0)
                    if not first:
                        pe.wait_ge(ada["got"], 2 * i + (8 + j - 1))
                    ada_unit(n + 1, i, 6 + j, ada["done"])

            up1_round(0, True)
            rounds(pe, 1, FF // 2, up1_round)
            pe.wait_ge(up1["free"], FF)
            out_projection(down1, down1["free"], "down1", FF, HID, BOTH, 11, (down1, (4, 5)))
            pe.wait_ge(ada["got"], 8 + FF)
            for u in range(6):
                n = BASE["ada_tail"] + u
                begin(n)
                for q in range(2):
                    for k in range(KC):
                        last = mm(bank[:, 7, 4 * u + 2 * q:4 * u + 2 * q + 2], slot(n, (q * KC + k) * P, P),
                                  CS[:, k, :], k == 0, k == KC - 1, q == 0 and k == 0)
            last.then_inc(ada["tail"], 1)
            norm_sums(na, BOTH)

            for b in range(21):
                n = BASE["proj"] + b // 2
                s = b % 3
                parts = LAT if b < 4 or 12 <= b < 18 else BOTH
                if b % 2 == 0:
                    begin(n)
                if b >= 3:
                    pe.wait_ge(proj["dve"] if (b - 3) % 2 else proj["act"], (b - 3) // 2 + 1)
                m = QK_D if b == 20 else P
                for k in range(KC):
                    if b == 0:
                        pe.wait_ge(na["ready"], 2 * (k + 1))
                    w = slot(n, ((b % 2) * KC + k) * P, P) if b < 20 else slot(n, k * QK_D, QK_D)
                    for x, y, c in parts:
                        last = mm(bank[0:m, 2 * s + c, 0:y - x], w, H[:, k, x:y], k == 0, k == KC - 1,
                                  b % 2 == 0 and k == 0 and c == 0)
                last.then_inc(proj["done"], 1)

            pe.wait_ge(proj["act"], 11)
            pe.wait_ge(proj["dve"], 10)
            for v in range(10):
                if v >= 4:
                    pe.wait_ge(vt["dve"] if v % 2 else vt["act"], (v - 4) // 2 + 1)
                for c in range(4):
                    last = nc.tensor.transpose(bank[:, v % 4, c * P:(c + 1) * P], VA[:, c, v * P:(v + 1) * P], ident)
                last.then_inc(vt["done"], 1)
            pe.wait_ge(vt["act"], 5)
            pe.wait_ge(vt["dve"], 5)

            def na_scores(u):
                h, j = u // N_BLK, u % N_BLK
                e = NA_D * (h % 2)
                q = QA[e:e + NA_D, h // 2, j * P:(j + 1) * P]
                nc.tensor.matmul(bank[:, NA_S[u % 3], 0:256].rearrange("p (r w) -> p r w", w=K_COLS), q,
                                 grid_cols(KA[e:e + NA_D, h // 2, 0:S], K_START[j]), start=True, stop=True)
                return nc.tensor.matmul(bank[:, NA_S[u % 3], 256:512], q, KA[e:e + NA_D, h // 2, S:T],
                                        start=True, stop=True)

            def na_values(u):
                h, j = u // N_BLK, u % N_BLK
                e = NA_D * (h % 2)
                for c in range(4):
                    v = VN[:, 2 * j + c if c < 2 else 6 + c, NA_D * h:NA_D * (h + 1)]
                    last = nc.tensor.matmul(bank[e:e + NA_D, 4 + h % 2, j * P:(j + 1) * P], v,
                                            TMP[:, u % 2, c * P:(c + 1) * P], start=(c == 0), stop=(c == 3))
                return last

            attention(ana, NA_HEADS * N_BLK, 1, na_scores,
                      lambda u: [[SQ5[:, u % 3, c * P:(c + 1) * P] for c in range(4)]], na_values, 3, (2, 3), 2, N_BLK)

            for k in range(QR):
                pe.wait_ge(lora["sq"], k + 1)
                if k == 0:
                    pe.wait_ge(ana["oc"], NA_HEADS)
                nc.tensor.matmul(bank[:, 0, :], ones, SQ[:, k % 2, 0:S], start=(k == 0),
                                 stop=(k == QR - 1)).then_inc(lora["sq_used"], 1)
            for k in range(KVR):
                pe.wait_ge(lora["sq"], QR + k + 1)
                nc.tensor.matmul(bank[:, 1, :], ones, SQ[:, k % 2, 0:S], start=(k == 0), stop=(k == KVR - 1))
                nc.tensor.matmul(bank[:, 2, 0:CTX], ones, SQ[:, k % 2, S:T], start=(k == 0),
                                 stop=(k == KVR - 1)).then_inc(lora["sq_used"], 1)
            nc.tensor.matmul(bank[0:QK_D, 3, :], con("rot", 0, QK_D, QK_D), KR[0:QK_D, 0:S], start=True,
                             stop=True).then_inc(gen["kr"], 1)
            pe.wait_ge(lora["normed"], 1)
            for h in range(NA_HEADS):
                n = BASE["uq"] + h // 2
                if h % 2 == 0:
                    begin(n)
                if h >= 2:
                    pe.wait_ge(gen["qc"], h - 1)
                for k in range(QR):
                    last = mm(bank[0:QK_D, 4 + h % 2, :], slot(n, ((h % 2) * QR + k) * QK_D, QK_D), CQ[:, k, :],
                              k == 0, k == QR - 1, h % 2 == 0 and k == 0)
                last.then_inc(gen["q"], 1)
                if h >= 1:
                    if h >= 3:
                        pe.wait_ge(gen["q_roped"], h - 2)
                    pe.wait_ge(gen["qc"], h)
                    nc.tensor.matmul(bank[0:QK_D, 6 + (h - 1) % 2, :], con("rot", 0, QK_D, QK_D),
                                     QM[0:QK_D, h - 1, :], start=True, stop=True).then_inc(gen["rot"], 1)
            pe.wait_ge(gen["q_roped"], NA_HEADS - 2)
            pe.wait_ge(gen["qc"], NA_HEADS)
            nc.tensor.matmul(bank[0:QK_D, 7, :], con("rot", 0, QK_D, QK_D), QM[0:QK_D, 7, :], start=True,
                             stop=True).then_inc(gen["rot"], 1)
            n = BASE["ukv_k"]
            begin(n)
            pe.wait_ge(gen["kr_roped"], 1)
            for h in range(NA_HEADS):
                if h >= 2:
                    pe.wait_ge(gen["kc"], h - 1)
                for k in range(KVR):
                    w = slot(n, (h * KVR + k) * NOPE, NOPE)
                    mm(bank[0:NOPE, 2 * (h % 2), :], w, CKV[:, k, 0:S], k == 0, k == KVR - 1, h == 0 and k == 0)
                for k in range(KVR):
                    last = mm(bank[0:NOPE, 2 * (h % 2) + 1, 0:CTX], slot(n, (h * KVR + k) * NOPE, NOPE),
                              CKV[:, k, S:T], k == 0, k == KVR - 1)
                last.then_inc(gen["k"], 1)
            n = BASE["ukv_v"]
            begin(n)
            for t in range(6):
                if t >= 2:
                    pe.wait_ge(gen["vc"], t - 1)
                for k in range(KVR):
                    last = mm(bank[:, 4 + t % 2, :], CKV[:, k, t * P:(t + 1) * P], slot(n, k * 512, 512),
                              k == 0, k == KVR - 1, t == 0 and k == 0)
                last.then_inc(gen["v"], 1)
            pe.wait_ge(gen["kc"], NA_HEADS)
            pe.wait_ge(gen["vc"], 6)
            pe.wait_ge(gen["q_roped"], NA_HEADS)

            def mla_scores(u):
                h, b = u // 4, u % 4
                q = QM[0:QK_D, h, b * P:(b + 1) * P]
                nc.tensor.matmul(bank[:, 2 * (u % 2), :], q, KM[0:QK_D, h, 0:S], start=True, stop=True)
                return nc.tensor.matmul(bank[:, 2 * (u % 2) + 1, 0:CTX], q, KM[0:QK_D, h, S:T], start=True, stop=True)

            def mla_values(u):
                h, b = u // 4, u % 4
                e = V_D * (h % 2)
                for c in range(6):
                    last = nc.tensor.matmul(bank[e:e + V_D, 6 + h % 2, b * P:(b + 1) * P],
                                            VM[:, c, V_D * h:V_D * (h + 1)], TMP[:, u % 2, c * P:(c + 1) * P],
                                            start=(c == 0), stop=(c == 5))
                return last

            attention(amla, NA_HEADS * 4, 1, mla_scores,
                      lambda u: [[PM[:, u % 3, c * P:(c + 1) * P] for c in r] for r in (range(3), range(3, 6))],
                      mla_values, 2, (4, 5), 2, 4)

            pe.wait_ge(amla["oc"], NA_HEADS)
            merged(mrg1, "merge1", 4, QA, OM)
            pe.wait_ge(mrg1["free"], KC)
            out_projection(out1, out1["free"], "out1", KC, MR1, LAT, 16, (out1, (4, 5)))
            norm_sums(nb, LAT)

            def up2_round(i, first=False, n=BASE["up2"], count=RING):
                for j in range(count):
                    if not (first and j < 2):
                        pe.wait_ge(up2["free"], RING * i + (j - 1))
                    swiglu_up(up2, n + j, i, None, j % 2, LAT, nb["ready"], first and j == 0)

            up2_round(0, True)
            rounds(pe, 1, FF // RING, up2_round)
            for f in range(FF // RING * RING, FF):
                pe.wait_ge(up2["free"], f - 1)
                swiglu_up(up2, BASE["up2"] + f, 0, None, f % 2, LAT, None, False)
            pe.wait_ge(up2["free"], FF)
            out_projection(down2, down2["free"], "down2", FF, HID, LAT, 11, (down2, (4, 5)))
            norm_sums(nmix, LAT)

            for b in range(8):
                n = BASE["qk_m"] + b // 2
                if b % 2 == 0:
                    begin(n)
                if b >= 4:
                    pe.wait_ge(conv["mixed"], b - 3)
                for k in range(KC):
                    if b == 0:
                        pe.wait_ge(nmix["ready"], k + 1)
                    last = mm(bank[:, b % 4, :], slot(n, ((b % 2) * KC + k) * P, P), H[:, k, 0:S], k == 0,
                              k == KC - 1, b % 2 == 0 and k == 0)
                last.then_inc(conv["raw"], 1)
            pe.wait_ge(conv["mixed"], 8)
            for b in range(20):
                if b >= 4:
                    pe.wait_ge(prj2["dve"] if b % 2 else prj2["act"], (b - 4) // 2 + 1)
                n = BASE["v_m"] + b // 2
                if b % 2 == 0:
                    begin(n)
                if b < 8 or b >= 18:
                    for q in range(2):
                        tt = 2 * (b % 2) + q
                        for k in range(KC):
                            last = mm(bank[:, b % 4, q * 256:(q + 1) * 256], H[:, k, tt * P:(tt + 1) * P],
                                      slot(n, k * 256, 256), k == 0, k == KC - 1, b % 2 == 0 and q == 0 and k == 0)
                else:
                    for k in range(KC):
                        last = mm(bank[:, b % 4, :], slot(n, ((b % 2) * KC + k) * P, P), H[:, k, 0:S], k == 0,
                                  k == KC - 1, b % 2 == 0 and k == 0)
                last.then_inc(prj2["done"], 1)
            n = BASE["if_m"]
            begin(n)
            for k in range(KC):
                last = mm(bank[0:36, 6, :], slot(n, k * 36, 36), H[:, k, 0:S], k == 0, k == KC - 1, k == 0)
            last.then_inc(gate["pre"], 1)
            pe.wait_ge(prj2["act"], 10)
            pe.wait_ge(prj2["dve"], 10)

            def sw_scores(u):
                pair, blk = u // 4, u % 4
                lo = max(blk - 1, 0) * P
                for e in range(2):
                    last = nc.tensor.matmul(bank[:, 2 * (u % 3) + e, (P if blk == 0 else 0):2 * P],
                                            QS[64 * e:64 * e + 64, pair, blk * P:(blk + 1) * P],
                                            KS[64 * e:64 * e + 64, pair // 2, lo:(blk + 1) * P],
                                            start=True, stop=True)
                return last

            def sw_pieces(u):
                blk = u % 4
                return [[SQ5[:, u % 3, (2 * e + c) * P:(2 * e + c + 1) * P] for e in range(2)
                         for c in range(1 if blk == 0 else 0, 2)]]

            def sw_values(u):
                pair, blk = u // 4, u % 4
                at = 0
                for e in range(2):
                    for c in range(1 if blk == 0 else 0, 2):
                        last = nc.tensor.matmul(bank[64 * e:64 * e + 64, 7, blk * P:(blk + 1) * P],
                                                VS[:, blk - 1 + c, 64 * (pair // 2):64 * (pair // 2) + 64],
                                                TMP5[:, u % 2, at * P:(at + 1) * P],
                                                start=(blk == 0 or c == 0), stop=(c == 1))
                        at += 1
                return last

            pe.wait_ge(gate["lf"], 1)
            attention(asw, 32, 2, sw_scores, sw_pieces, sw_values, 3, (6,), 1, 4)

            pe.wait_ge(asw["oc"], 8)
            pe.wait_ge(gate["rows"], 1)
            for c in range(4):
                last = nc.tensor.transpose(bank[:, 7, c * 4:(c + 1) * 4], ROWS[0:4, 2, c * P:(c + 1) * P],
                                           con("ident", 0, 4, 4))
            last.then_inc(gate["cols"], 1)
            pe.wait_ge(gate["ready"], 1)
            for h in range(X_HEADS):
                if h >= 1:
                    pe.wait_ge(ml["floor"], h)
                nc.tensor.matmul(bank[:, 0, :], con("select", h * P, P, 4), ROWS[0:4, 3, :], start=True, stop=True)
                nc.tensor.matmul(bank[:, 1, :], con("select", h * P, P, 4), ROWS[0:4, 4, :], start=True,
                                 stop=True).then_inc(ml["bcast"], 1)
                for c in range(5):
                    if c < 4:
                        if 4 * h + c >= 2:
                            pe.wait_ge(ml["w"], 4 * h + c - 1)
                        nc.tensor.matmul(bank[:, 2 + c % 2, 0:S - c * P], QK[:, 4 + h, c * P:(c + 1) * P],
                                         QK[:, h, c * P:S], start=True, stop=True).then_inc(ml["s"], 1)
                    if c >= 1:
                        d = c - 1
                        pe.wait_ge(ml["w"], 4 * h + d + 1)
                        if d == 0 and h >= 1:
                            pe.wait_ge(ml["num"], h)
                        for v in range(2):
                            nc.tensor.matmul(bank[:, 4 + v, d * P:S], VX[:, d, (2 * h + v) * P:(2 * h + v + 1) * P],
                                             TMP5[:, d % 2, 0:S - d * P], start=(d == 0), stop=(d == 3))
                        nc.tensor.matmul(bank[:, 6, d * P:S], ones, TMP5[:, d % 2, 0:S - d * P], start=(d == 0),
                                         stop=(d == 3)).then_inc(ml["used"], 1)
                for v in range(2):
                    pe.wait_ge(ml["sq"], 2 * h + v + 1)
                    last = nc.tensor.matmul(bank[:, 7, :], ones, SQ5[:, v, :], start=(v == 0), stop=(v == 1))
                last.then_inc(ml["ssq"], 1)
            pe.wait_ge(ml["root"], X_HEADS)

            for b in range(8):
                n = BASE["o_m"] + b // 2
                if b % 2 == 0:
                    begin(n)
                if b >= 2:
                    pe.wait_ge(og["act"], b - 1)
                for k in range(KC):
                    last = mm(bank[:, 2 + b % 2, :], slot(n, ((b % 2) * KC + k) * P, P), H[:, k, 0:S], k == 0,
                              k == KC - 1, b % 2 == 0 and k == 0)
                last.then_inc(og["done"], 1)
            pe.wait_ge(og["free"], 8)
            merged(mrg2, "merge2", 8, YA, QS)
            pe.wait_ge(mrg2["free"], 2 * KC)
            out_projection(out2, nmlp["xnew"], "out2", KC, MR2, LAT, 16, (nmlp, (6,)))

            def up3_round(i, first=False):
                for j in range(8):
                    n = BASE["up3"] + j // 2
                    if j % 2 == 0:
                        begin(n, i)
                    if not (first and j < 4):
                        pe.wait_ge(up3["free"], 8 * i + (j - 3))
                    for k in range(KC):
                        if first and j == 0:
                            pe.wait_ge(nmlp["ready"], nmlp["base"] + k + 1)
                        last = mm(bank[:, j % 4, :], slot(n, ((j % 2) * KC + k) * P, P), H[:, k, 0:S], k == 0,
                                  k == KC - 1, j % 2 == 0 and k == 0)
                    last.then_inc(up3["done"], 1)

            up3_round(0, True)
            rounds(pe, 1, FF2 // 8, up3_round)
            pe.wait_ge(up3["free"], FF2)
            out_projection(down3, nple["xnew"], "down3", FF2, HID2, LAT, 16, (nple, (6,)))

            for o in range(KC):
                n = BASE["ple"] + o
                s = o % 2
                begin(n)
                if o >= 2:
                    pe.wait_ge(ple["free"], o - 1)
                for k in range(KC):
                    if o == 0:
                        pe.wait_ge(nple["ready"], nple["base"] + k + 1)
                    mm(bank[:, 2 * s, :], slot(n, k * P, P), H[:, k, 0:S], k == 0, k == KC - 1, k == 0)
                for k in range(2):
                    last = mm(bank[:, 2 * s + 1, :], slot(n, (KC + k) * P, P), PE2[:, k, :], k == 0, k == 1)
                last.then_inc(ple["done"], 1)
                if o >= 1:
                    sum_squares(nfin, o - 1, LAT, (6,)).then_inc(nfin["sq_used"], 1)
            sum_squares(nfin, KC - 1, LAT, (6,)).then_inc(nfin["sq_used"], 1)

        @block.scalar
        def _(act):
            A = nc.scalar.activation
            act.dma_start(CVEC, cT).then_inc(inputs_landed, 16)
            act.dma_start(prm[:, :], params).then_inc(inputs_landed, 16)
            act.dma_start(X[:, 0:4, :], xT[:, 0:4, :]).then_inc(inputs_landed, 16)
            act.dma_start(X[:, 4:8, :], xT[:, 4:8, :]).then_inc(inputs_landed, 16)
            act.dma_start(cst[:, :], consts).then_inc(inputs_landed, 16)
            act.dma_start(PE2, pT).then_inc(inputs_landed, 16)
            act.dma_start(bias_t[:, :], rpb).then_inc(rpb_landed, 16)

            def norm_squares(g, width, per_chunk):
                for k in range(KC):
                    if per_chunk:
                        act.wait_ge(g["xnew"], g["base"] + per_chunk * (k + 1))
                    if k >= 2:
                        act.wait_ge(g["sq_used"], g["base"] + k - 1)
                    A(SQ[:, k % 2, 0:width], X[:, k, 0:width], ACT.Square).then_inc(g["sq"], 1)

            def root(g, parts, banks, signal, features):
                for (a, b, _), n in zip(parts, banks):
                    A(rs[:, a:b], bank[:, n, 0:b - a], ACT.Sqrt, bias=eps, scale=1.0 / features).then_inc(signal, 1)

            def norm(g, parts, shift):
                act.wait_ge(g["sq_used"], g["base"] + KC)
                root(g, parts, (6, 5), g["root"], D)
                if shift is not None:
                    for k in range(KC):
                        for c, (a, b, col) in enumerate(parts):
                            act.wait_ge(g["scaled"], len(parts) * k + c + 1)
                            A(H[:, k, a:b], H[:, k, a:b], ACT.Identity,
                              bias=MODS[:, shift * KC + k, col:col + 1]).then_inc(g["ready"], 1)

            def post_norm(g, prev, parts):
                act.wait_ge(prev["sq_used"], prev["base"] + KC)
                root(g, parts, (4, 5), g["y_root"], D)
                norm_squares(g, parts[-1][1], len(parts))

            def swiglu(g, f, j, parts, peeled):
                act.wait_ge(g["done"], f + 1)
                if not peeled:
                    act.wait_ge(g["free"], f - 1)
                A(TMP[:, j, 0:S], bank[:, 3 * j, :], ACT.Silu).then_inc(g["act"], 1)
                if len(parts) == 2:
                    A(TMP[:, j, S:T], bank[:, 3 * j + 2, 0:CTX], ACT.Silu).then_inc(g["act"], 1)

            def down_out(g, o, j, parts, peeled):
                act.wait_ge(g["done"], o + (g["base"] + 1))
                if not peeled:
                    act.wait_ge(g["sq_used"], o + (g["base"] - 1))
                for a, b, c in parts:
                    last = A(SQ[:, j, a:b], bank[:, 2 * j + c, 0:b - a], ACT.Square)
                last.then_inc(g["sq"], 1)
                for a, b, c in parts:
                    dst = H[:, o, a:b] if isinstance(o, int) else \
                        H[:, bass.ds(o, 1), a:b].rearrange("p o t -> p (o t)")
                    last = A(dst, bank[:, 2 * j + c, 0:b - a], ACT.Copy)
                last.then_inc(g["free"], 1)

            def down(g, parts):
                def body(i, peeled=False):
                    for j in range(2):
                        down_out(g, 2 * i + j, j, parts, peeled)
                body(0, True)
                rounds(act, 1, KC // 2, body)

            def merge_gates(g, bias):
                for o in range(KC):
                    s = o % 2
                    act.wait_ge(g["done"], g["base"] + o + 1)
                    if o >= 2:
                        act.wait_ge(g["free"], g["base"] + o - 1)
                    for q, dst in ((0, SQ5), (1, TMP5)):
                        b = par("b_gate", q * KC + o) if bias else 0.0
                        A(dst[:, s, :], bank[:, 4 * s + q, :], ACT.Sigmoid, bias=b).then_inc(g["gate"], 1)

            def attention(g, units, exp_rows, pieces, turned_to, t_banks):
                upto = [0]
                for u in range(units):
                    upto.append(upto[-1] + len(pieces(u)))
                for i in range(units + 2):
                    if i < units:
                        act.wait_ge(g["max"], i + 1)
                        if i >= 3:
                            act.wait_ge(g["t"], upto[i - 2])
                        exp_rows(i)
                    if i >= 2:
                        u = i - 2
                        if u >= 2:
                            act.wait_ge(g["pv"], u - 1)
                        for q, width in enumerate(pieces(u)):
                            n = upto[u] + q
                            act.wait_ge(g["t"], n + 1)
                            A(turned_to(u, q, width), bank[:, t_banks[n % len(t_banks)], 0:width],
                              ACT.Copy).then_inc(g["tc"], 1)

            act.wait_ge(inputs_landed, 16 * N_LOADS)
            A(cs[:, :], cvec[:, :], ACT.Silu).then_inc(ada["silu"], 1)
            norm_squares(n0, T, 0)
            norm(n0, BOTH, 0)

            def up1_act(i, peeled=False):
                for j in range(2):
                    swiglu(up1, 2 * i + j, j, BOTH, peeled)
            up1_act(0, True)
            rounds(act, 1, FF // 2, up1_act)
            act.wait_ge(up1["free"], FF)
            down(down1, BOTH)
            post_norm(na, down1, BOTH)
            act.wait_ge(ada["tail_got"], 1)
            norm(na, BOTH, 3)

            def proj_out(b):
                m = QK_D if b == 20 else P
                s = b % 3
                if b < 4:
                    return [q_blocks(b)]
                if 8 <= b < 12:
                    return v_blocks(b)
                if 12 <= b < 18:
                    return [(CQ[:, b - 12, :], bank[:, 2 * s, :])]
                dst = KR[0:m, :] if b == 20 else (KA if b < 8 else CKV)[:, b % 4 if b < 12 else b - 18, :]
                return [(dst[:, 0:S], bank[0:m, 2 * s, :]), (dst[:, S:T], bank[0:m, 2 * s + 1, 0:CTX])]

            for b in range(0, 21, 2):
                act.wait_ge(proj["done"], b + 1)
                pairs = proj_out(b)
                for dst, src in pairs:
                    last = A(dst, src, ACT.Copy, scale=NA_D ** -0.5 if b < 4 else 1.0)
                last.then_inc(proj["act"], 1)
            for v in range(0, 10, 2):
                act.wait_ge(vt["done"], v + 1)
                A(VN[:, v, :], bank[:, v % 4, :], ACT.Copy).then_inc(vt["act"], 1)

            def stat_col(u, i, n=1):
                return stat[:, 16 * (u % 4) + i:16 * (u % 4) + i + n]

            def na_exp(u):
                A(SQ5[:, u % 3, :], bank[:, NA_S[u % 3], :], ACT.Exp, bias=stat_col(u, 0),
                  accum_out=stat_col(u, 2)).then_inc(ana["exp"], 1)

            attention(ana, NA_HEADS * N_BLK, na_exp, lambda u: [512], lambda u, q, w: TMP[:, u % 2, 0:w], (2, 3))

            act.wait_ge(proj["dve"], 10)
            act.wait_ge(ana["t"], NA_HEADS * N_BLK)
            for k in range(QR + KVR):
                if k >= 2:
                    act.wait_ge(lora["sq_used"], k - 1)
                src, w = (CQ[:, k, :], S) if k < QR else (CKV[:, k - QR, :], T)
                A(SQ[:, k % 2, 0:w], src, ACT.Square).then_inc(lora["sq"], 1)
            act.wait_ge(lora["sq_used"], QR)
            act.wait_ge(ana["pv"], NA_HEADS * N_BLK)
            A(TMP[:, 0, 0:S], bank[:, 0, :], ACT.Sqrt, bias=eps, scale=1.0 / ML_Q_RANK).then_inc(lora["root"], 1)
            act.wait_ge(lora["sq_used"], QR + KVR)
            A(rs[:, 0:S], bank[:, 1, :], ACT.Sqrt, bias=eps, scale=1.0 / ML_KV_RANK).then_inc(lora["root"], 1)
            A(rs[:, S:T], bank[:, 2, 0:CTX], ACT.Sqrt, bias=eps, scale=1.0 / ML_KV_RANK).then_inc(lora["root"], 1)
            act.wait_ge(ana["oc"], NA_HEADS)
            for h in range(NA_HEADS):
                act.wait_ge(gen["q"], h + 1)
                A(QM[0:QK_D, h, :], bank[0:QK_D, 4 + h % 2, :], ACT.Copy, scale=QK_D ** -0.5).then_inc(gen["qc"], 1)
            for h in range(NA_HEADS):
                act.wait_ge(gen["k"], h + 1)
                A(KM[0:NOPE, h, 0:S], bank[0:NOPE, 2 * (h % 2), :], ACT.Copy)
                A(KM[0:NOPE, h, S:T], bank[0:NOPE, 2 * (h % 2) + 1, 0:CTX], ACT.Copy).then_inc(gen["kc"], 1)

            def mla_exp(u):
                s = u % 2
                A(PM[:, u % 3, :], bank[:, 2 * s:2 * s + 2, :].rearrange("p a b -> p (a b)")[:, 0:T], ACT.Exp,
                  bias=stat_col(u, 0), accum_out=stat_col(u, 2)).then_inc(amla["exp"], 1)

            attention(amla, NA_HEADS * 4, mla_exp, lambda u: [384, 384],
                      lambda u, q, w: TMP[:, u % 2, q * w:(q + 1) * w], (4, 5))
            act.wait_ge(amla["pv"], NA_HEADS * 4)
            merge_gates(mrg1, True)
            act.wait_ge(mrg1["free"], KC)
            down(out1, LAT)
            post_norm(nb, out1, LAT)
            norm(nb, LAT, 6)

            def up2_act(i, peeled=False):
                for j in range(2):
                    swiglu(up2, 2 * i + j, j, LAT, peeled)
            up2_act(0, True)
            rounds(act, 1, FF // 2, up2_act)
            act.wait_ge(up2["free"], FF)
            down(down2, LAT)
            post_norm(nmix, down2, LAT)
            norm(nmix, LAT, None)

            for b in range(8):
                act.wait_ge(conv["mixed"], b + 1)
                A(QK[:, b, :], TMP5[:, b % 2, :], ACT.Silu).then_inc(conv["ready"], 1)
            for b in range(0, 20, 2):
                act.wait_ge(prj2["done"], b + 1)
                if b < 8:
                    A(VX[:, 0:2, (b // 2) * 256:(b // 2 + 1) * 256],
                      bank[:, b % 4, :].rearrange("p (t n) -> p t n", t=2), ACT.Copy).then_inc(prj2["act"], 1)
                elif b < 16:
                    A(QS[:, b - 8, :], bank[:, b % 4, :], ACT.Copy, scale=SW_D ** -0.5).then_inc(prj2["act"], 1)
                elif b == 16:
                    for q in range(4):
                        last = A(KS[64 * (q // 2):64 * (q // 2) + 64, q % 2, :],
                                 bank[64 * (q % 2):64 * (q % 2) + 64, b % 4, :], ACT.Copy)
                    last.then_inc(prj2["act"], 1)
                else:
                    A(VS[:, 0:2, :], bank[:, b % 4, :].rearrange("p (t n) -> p t n", t=2),
                      ACT.Copy).then_inc(prj2["act"], 1)

            def sw_exp(u):
                s, lo = u % 3, (P if u % 4 == 0 else 0)
                for e in range(2):
                    A(SQ5[:, s, e * 256 + lo:(e + 1) * 256], bank[:, 2 * s + e, lo:256], ACT.Exp,
                      bias=stat_col(u, e), accum_out=stat_col(u, 2 + e)).then_inc(asw["exp"], 1)
                A(stat_col(u, 6, 2), stat_col(u, 4, 2), ACT.Exp).then_inc(asw["biased"], 1)

            attention(asw, 32, sw_exp, lambda u: [256 if u % 4 == 0 else 512],
                      lambda u, q, w: TMP5[:, u % 2, 0:w], (6,))

            act.wait_ge(gate["lf"], 2)
            A(ROWS[0:4, 5, :], ROWS[0:4, 5, :], ACT.Exp, scale=-1.0).then_inc(gate["exp"], 1)
            act.wait_ge(gate["exp"], 1)
            A(ROWS[0:4, 5, :], ROWS[0:4, 5, :], ACT.Ln, bias=con("ones", 0, 1, 4)).then_inc(gate["soft"], 1)
            for h in range(X_HEADS):
                act.wait_ge(ml["bcast"], h + 1)
                if h == 0:
                    act.wait_ge(gate["ready"], 1)
                A(rs[:, 0:S], bank[:, 0, :], ACT.Copy, scale=-1.0).then_inc(ml["minus_m"], 1)
                for c in range(4):
                    n = 4 * h + c
                    act.wait_ge(ml["minus_m"], h + 1)
                    act.wait_ge(ml["diag"], n + 1)
                    if c < 3:
                        A(SQ5[:, c % 2, P:S - c * P], rs[:, (c + 1) * P:S], ACT.Exp, bias=ACOL[:, c, h:h + 1])
                    A(SQ5[:, c % 2, 0:P], SQ5[:, c % 2, 0:P], ACT.Exp, bias=ACOL[:, c, h:h + 1]).then_inc(ml["e"], 1)
                act.wait_ge(ml["w"], 4 * h + 4)
                A(SQ5[:, 2, :], bank[:, 1, :], ACT.Exp, scale=-1.0).then_inc(ml["floor"], 1)
                act.wait_ge(ml["used"], 4 * h + 4)
                A(TMP5[:, 2, :], bank[:, 6, :], ACT.Abs).then_inc(ml["acc"], 1)
                for v in range(2):
                    act.wait_ge(ml["num"], h + 1)
                    A(SQ5[:, v, :], YA[:, 2 * h + v, :], ACT.Square).then_inc(ml["sq"], 1)
                act.wait_ge(ml["ssq"], h + 1)
                A(rs[:, 0:S], bank[:, 7, :], ACT.Sqrt, bias=eps, scale=1.0 / X_DV).then_inc(ml["root"], 1)
                act.wait_ge(ml["head"], h + 1)
            for b in range(8):
                act.wait_ge(og["done"], b + 1)
                if b >= 2:
                    act.wait_ge(og["free"], b - 1)
                A(TMP5[:, b % 2, :], bank[:, 2 + b % 2, :], ACT.Sigmoid).then_inc(og["act"], 1)
            act.wait_ge(og["free"], 8)
            merge_gates(mrg2, False)
            act.wait_ge(mrg2["free"], 2 * KC)
            norm_squares(nmlp, S, 1)
            norm(nmlp, LAT, None)

            def up3_act(i, peeled=False):
                for j in range(8):
                    act.wait_ge(up3["done"], 8 * i + j + 1)
                    dst = HID2[:, 8 * i + j, :] if isinstance(i, int) else \
                        HID2[:, bass.ds(8 * i + j, 1), :].rearrange("p o t -> p (o t)")
                    A(dst, bank[:, j % 4, :], ACT.Relu).then_inc(up3["act"], 1)
            rounds(act, 0, FF2 // 8, up3_act)
            norm_squares(nple, S, 1)
            norm(nple, LAT, None)

            for o in range(KC + 1):
                if o < KC:
                    act.wait_ge(ple["done"], o + 1)
                    if o >= 2:
                        act.wait_ge(nfin["xnew"], nfin["base"] + o - 1)
                    A(TMP5[:, o % 2, :], bank[:, 2 * (o % 2), :], ACT.Sigmoid).then_inc(ple["gate"], 1)
                if o >= 1:
                    k = o - 1
                    act.wait_ge(nfin["xnew"], nfin["base"] + k + 1)
                    if k >= 2:
                        act.wait_ge(nfin["sq_used"], nfin["base"] + k - 1)
                    A(SQ[:, k % 2, 0:S], X[:, k, 0:S], ACT.Square).then_inc(nfin["sq"], 1)
            norm(nfin, LAT, None)

        @block.vector
        def _(dve):
            V = nc.vector
            chain = [0]

            def link(ins):
                chain[0] += 1
                ins.then_inc(dve_c, 1)
                dve.wait_ge(dve_c, chain[0])

            def mark(ins):
                chain[0] += 1
                ins.then_inc(dve_c, 1)
                return chain[0]

            def norm(g, parts, scale, shifted):
                dve.wait_ge(g["root"], g["turn"] + len(parts))
                width = parts[-1][1]
                link(V.reciprocal(rs[:, 0:width], rs[:, 0:width]))
                for k in range(KC):
                    for a, b, col in parts:
                        V.scalar_tensor_tensor(H[:, k, a:b], X[:, k, a:b], scale(k, col), rs[:, a:b], ALU.mult,
                                               ALU.mult).then_inc(g["scaled"] if shifted else g["ready"], 1)

            def post_norm(g, parts, gate_row):
                dve.wait_ge(g["y_root"], len(parts))
                width = parts[-1][1]
                link(V.reciprocal(rs[:, 0:width], rs[:, 0:width]))
                marks = {}
                for k in range(KC + 1):
                    if k < KC:
                        if k >= 2:
                            dve.wait_ge(g["xnew"], len(parts) * (k - 1))
                        for a, b, col in parts:
                            marks[k, col] = mark(V.scalar_tensor_tensor(
                                TMP[:, k % 2, a:b], H[:, k, a:b], COEF[:, gate_row, k, col:col + 1], rs[:, a:b],
                                ALU.mult, ALU.mult))
                    if k >= 1:
                        for a, b, col in parts:
                            dve.wait_ge(dve_c, marks[k - 1, col])
                            V.tensor_tensor(X[:, k - 1, a:b], X[:, k - 1, a:b], TMP[:, (k - 1) % 2, a:b],
                                            ALU.add).then_inc(g["xnew"], 1)

            def modulated(row):
                return lambda k, col: COEF[:, row, k, col:col + 1]

            def plain(name):
                return lambda k, col: par(name, k)

            def mods_of(i):
                return MODS[:, i * KC:(i + 1) * KC, :]

            def norm_g(i):
                return par("norm_g", i * 2 * KC, 2 * KC).rearrange("p (k c) -> p k c", c=2)

            def scale_coef(row, m, g):
                return V.scalar_tensor_tensor(COEF[:, row, :, :], mods_of(m), 1.0, norm_g(g), ALU.add, ALU.mult)

            def gate_coef(row, m, weight, g):
                return V.scalar_tensor_tensor(COEF[:, row, :, :], mods_of(m), weight, norm_g(g), ALU.mult, ALU.mult)

            def ada_out(u, b):
                dve.wait_ge(ada["done"], u + 1)
                if isinstance(u, int):
                    dst, bias = mods_t[:, 4 * u:4 * u + 4], par("b_ada", 4 * u, 4)
                else:
                    dst, bias = mods_t[:, bass.ds(4 * u, 4)], prm[:, bass.ds(4 * u + PARAM["b_ada"], 4)]
                return V.tensor_tensor(dst, bank[:, b, 0:4], bias, ALU.add).then_inc(ada["got"], 1)

            def product(g, f, j, parts):
                def hid(a, b):
                    return HID[:, f, a:b] if isinstance(f, int) else \
                        HID[:, bass.ds(f, 1), a:b].rearrange("p o t -> p (o t)")
                n = len(parts)
                dve.wait_ge(g["act"], n * f + 1)
                if n == 2:
                    V.tensor_tensor(hid(0, S), TMP[:, j, 0:S], bank[:, 3 * j + 1, :], ALU.mult)
                    dve.wait_ge(g["act"], n * f + 2)
                    V.tensor_tensor(hid(S, T), TMP[:, j, S:T], bank[:, 3 * j + 2, CTX:2 * CTX],
                                    ALU.mult).then_inc(g["free"], 1)
                else:
                    V.tensor_tensor(hid(0, S), TMP[:, j, 0:S], bank[:, 3 * j + 1, :], ALU.mult).then_inc(g["free"], 1)

            def residual_add(g, done, o, j):
                dve.wait_ge(done, o + (g["base"] + 1))
                x = X[:, o, 0:S] if isinstance(o, int) else X[:, bass.ds(o, 1), 0:S].rearrange("p o t -> p (o t)")
                V.tensor_tensor(x, x, bank[:, 2 * j, :], ALU.add).then_inc(g["xnew"], 1)

            def residual_adds(g, done):
                def body(i):
                    for j in range(2):
                        residual_add(g, done, 2 * i + j, j)
                rounds(dve, 0, KC // 2, body)

            def merge(g, dst):
                for o in range(KC):
                    s = o % 2
                    dve.wait_ge(g["gate"], 2 * (g["base"] + o) + 1)
                    mark(V.tensor_tensor(SQ5[:, s, :], SQ5[:, s, :], bank[:, 4 * s + 2, :], ALU.mult))
                    dve.wait_ge(g["gate"], 2 * (g["base"] + o) + 2)
                    link(V.tensor_tensor(TMP5[:, s, :], TMP5[:, s, :], bank[:, 4 * s + 3, :], ALU.mult))
                    V.tensor_tensor(dst[:, o, :], SQ5[:, s, :], TMP5[:, s, :], ALU.add).then_inc(g["free"], 1)

            def stat_col(u, i, n=1):
                return stat[:, 16 * (u % 4) + i:16 * (u % 4) + i + n]

            def attention(g, units, maxima, normalise, per_out, take):
                for i in range(units + 4):
                    u = i - 4
                    if u >= 0 and u % per_out == per_out - 1:
                        dve.wait_ge(g["pv"], u + 1)
                        take(u // per_out).then_inc(g["oc"], 1)
                    if i < units:
                        dve.wait_ge(g["s"], i + 1)
                        maxima(i)
                    if 1 <= i <= units:
                        normalise(i - 1)

            dve.wait_ge(inputs_landed, 16 * N_LOADS)
            for u in range(8):
                ada_out(u, u % 2)
            dve.wait_ge(ada["got"], 8)
            link(scale_coef(SCALE1, 1, 0))
            norm(n0, BOTH, modulated(SCALE1), True)

            def up1_dve(i):
                for j in range(2):
                    product(up1, 2 * i + j, j, BOTH)
                    ada_out(2 * i + (8 + j), 6 + j)
            rounds(dve, 0, FF // 2, up1_dve)
            dve.wait_ge(ada["got"], 8 + FF)
            mark(gate_coef(GATE1, 2, 0.5, 1))
            mark(scale_coef(SCALE2, 4, 2))
            link(gate_coef(GATE2, 5, 1.0, 3))
            dve.wait_ge(down1["free"], KC)
            post_norm(na, BOTH, GATE1)
            dve.wait_ge(ada["tail"], 1)
            V.tensor_tensor(mods_t[:, 4 * 30:4 * 36], bank[:, 7, 0:24], par("b_ada", 120, 24),
                            ALU.add).then_inc(ada["tail_got"], 1)
            dve.wait_ge(ada["tail_got"], 1)
            mark(scale_coef(SCALE3, 7, 4))
            link(gate_coef(GATE3, 8, 0.5, 5))
            norm(na, BOTH, modulated(SCALE2), True)

            for b in range(1, 21, 2):
                dve.wait_ge(proj["done"], b + 1)
                s = b % 3
                if b < 4:
                    dst, src = q_blocks(b)
                    V.tensor_scalar(dst, src, NA_D ** -0.5, None, ALU.mult).then_inc(proj["dve"], 1)
                elif 8 <= b < 12:
                    for dst, src in v_blocks(b):
                        ins = V.tensor_copy(dst, src)
                    ins.then_inc(proj["dve"], 1)
                elif 12 <= b < 18:
                    V.tensor_copy(CQ[:, b - 12, :], bank[:, 2 * s, :]).then_inc(proj["dve"], 1)
                else:
                    dst = (KA if b < 8 else CKV)[:, b % 4 if b < 12 else b - 18, :]
                    mark(V.tensor_copy(dst[:, 0:S], bank[:, 2 * s, :]))
                    V.tensor_copy(dst[:, S:T], bank[:, 2 * s + 1, 0:CTX]).then_inc(proj["dve"], 1)
            for v in range(1, 10, 2):
                dve.wait_ge(vt["done"], v + 1)
                V.tensor_copy(VN[:, v, :], bank[:, v % 4, :]).then_inc(vt["dve"], 1)

            def na_maxima(u):
                dve.wait_ge(ana["bias"], u + 1)
                ins = V.tensor_tensor(bank[:, NA_S[u % 3], 0:256], bank[:, NA_S[u % 3], 0:256],
                                      bm_t[:, 256 * (u % 2):256 * (u % 2) + 256], ALU.add)
                ins.then_inc(ana["biased"], 1)
                dve.wait_ge(ana["biased"], u + 1)
                V.tensor_reduce(stat_col(u, 0), bank[:, NA_S[u % 3], :], AX.X, ALU.max, negate=True).then_inc(ana["max"], 1)

            def plain_normalise(g, rows, width):
                def run(u):
                    dve.wait_ge(g["exp"], u + 1)
                    link(V.reciprocal(stat_col(u, 3), stat_col(u, 2)))
                    V.tensor_scalar(rows[:, u % 3, 0:width], rows[:, u % 3, 0:width], stat_col(u, 3), None,
                                    ALU.mult).then_inc(g["norm"], 1)
                return run

            def na_take(h):
                e = NA_D * (h % 2)
                dst = QA[e:e + NA_D, h // 2, :].rearrange("p (r j c) -> p j r c", r=GRID_H, j=N_BLK)
                src = bank[e:e + NA_D, 4 + h % 2, :].rearrange("p (j r c) -> p j r c", j=N_BLK, r=GRID_H)
                return V.tensor_copy(dst, src)

            attention(ana, NA_HEADS * N_BLK, na_maxima, plain_normalise(ana, SQ5, 512), N_BLK, na_take)

            dve.wait_ge(gen["kr"], 1)
            dve.wait_ge(lora["root"], 1)
            link(V.reciprocal(TMP[:, 0, 0:S], TMP[:, 0, 0:S]))
            for k in range(QR):
                mark(V.scalar_tensor_tensor(CQ[:, k, :], CQ[:, k, :], par("g_q", k), TMP[:, 0, 0:S], ALU.mult,
                                            ALU.mult))
            dve.wait_ge(lora["root"], 3)
            link(V.reciprocal(rs[:, :], rs[:, :]))
            for k in range(KVR):
                last = V.scalar_tensor_tensor(CKV[:, k, :], CKV[:, k, :], par("g_kv", k), rs[:, :], ALU.mult, ALU.mult)
                if k < KVR - 1:
                    mark(last)
            last.then_inc(lora["normed"], 1)
            dve.wait_ge(lora["normed"], 1)
            mark(V.tensor_tensor(TMP[0:QK_D, 1, 0:S], bank[0:QK_D, 3, :], con("sin", 0, S, QK_D), ALU.mult))
            link(V.tensor_tensor(KR[0:QK_D, 0:S], KR[0:QK_D, 0:S], con("cos", 0, S, QK_D), ALU.mult))
            link(V.tensor_tensor(KR[0:QK_D, 0:S], KR[0:QK_D, 0:S], TMP[0:QK_D, 1, 0:S], ALU.add))
            for h in range(NA_HEADS):
                last = V.tensor_copy(KM[NOPE:QK_D, h, :], KR[NOPE:QK_D, :])
                if h < NA_HEADS - 1:
                    mark(last)
            last.then_inc(gen["kr_roped"], 1)
            for h in range(NA_HEADS):
                dve.wait_ge(gen["rot"], h + 1)
                mark(V.tensor_tensor(TMP5[0:QK_D, h % 2, :], bank[0:QK_D, 6 + h % 2, :], con("sin", 0, S, QK_D),
                                     ALU.mult))
                link(V.tensor_tensor(QM[0:QK_D, h, :], QM[0:QK_D, h, :], con("cos", 0, S, QK_D), ALU.mult))
                V.tensor_tensor(QM[0:QK_D, h, :], QM[0:QK_D, h, :], TMP5[0:QK_D, h % 2, :],
                                ALU.add).then_inc(gen["q_roped"], 1)
            for t in range(6):
                dve.wait_ge(gen["v"], t + 1)
                V.tensor_copy(VM[:, t, :], bank[:, 4 + t % 2, :]).then_inc(gen["vc"], 1)

            def mla_maxima(u):
                s = u % 2
                V.tensor_reduce(stat_col(u, 0), bank[:, 2 * s:2 * s + 2, :].rearrange("p a b -> p (a b)")[:, 0:T],
                                AX.X, ALU.max, negate=True).then_inc(amla["max"], 1)

            def mla_take(h):
                e = V_D * (h % 2)
                return V.tensor_copy(OM[e:e + V_D, h // 2, :], bank[e:e + V_D, 6 + h % 2, :])

            attention(amla, NA_HEADS * 4, mla_maxima, plain_normalise(amla, PM, T), 4, mla_take)
            merge(mrg1, MR1)
            dve.wait_ge(out1["free"], 2 * KC)
            post_norm(nb, LAT, GATE2)
            norm(nb, LAT, modulated(SCALE3), True)

            def up2_dve(i):
                for j in range(2):
                    product(up2, 2 * i + j, j, LAT)
            rounds(dve, 0, FF // 2, up2_dve)
            dve.wait_ge(down2["free"], 3 * KC)
            post_norm(nmix, LAT, GATE3)
            norm(nmix, LAT, plain("mix_g"), False)

            for b in range(8):
                dve.wait_ge(conv["raw"], b + 1)
                if b >= 2:
                    dve.wait_ge(conv["ready"], b - 1)
                acc = TMP5[:, b % 2, :]
                link(V.tensor_scalar(acc, bank[:, b % 4, :], par("conv", 4 * b + 3), None, ALU.mult))
                for back in range(1, 4):
                    ins = V.scalar_tensor_tensor(acc[:, back:S], bank[:, b % 4, 0:S - back],
                                                 par("conv", 4 * b + 3 - back), acc[:, back:S], ALU.mult, ALU.add)
                    if back < 3:
                        link(ins)
                ins.then_inc(conv["mixed"], 1)
            for b in range(1, 20, 2):
                dve.wait_ge(prj2["done"], b + 1)
                if b < 8:
                    V.tensor_copy(VX[:, 2:4, (b // 2) * 256:(b // 2 + 1) * 256],
                                  bank[:, b % 4, :].rearrange("p (t n) -> p t n", t=2)).then_inc(prj2["dve"], 1)
                elif b < 16:
                    V.tensor_scalar(QS[:, b - 8, :], bank[:, b % 4, :], SW_D ** -0.5, None,
                                    ALU.mult).then_inc(prj2["dve"], 1)
                elif b == 17:
                    for q in range(4):
                        ins = V.tensor_copy(KS[64 * (q // 2):64 * (q // 2) + 64, 2 + q % 2, :],
                                            bank[64 * (q % 2):64 * (q % 2) + 64, b % 4, :])
                        if q < 3:
                            mark(ins)
                    ins.then_inc(prj2["dve"], 1)
                else:
                    V.tensor_copy(VS[:, 2:4, :], bank[:, b % 4, :].rearrange("p (t n) -> p t n", t=2)
                                  ).then_inc(prj2["dve"], 1)
            dve.wait_ge(gate["pre"], 1)
            mark(V.tensor_scalar(YA[0:4, 0, :], bank[0:4, 6, :], par("b_if", 0, 1, 4), None, ALU.add))
            V.tensor_scalar(YA[0:4, 1, :], bank[32:36, 6, :], prm[32:36, PARAM["b_if"] + 1:PARAM["b_if"] + 2],
                            None, ALU.add).then_inc(gate["lf"], 1)

            def sw_maxima(u):
                s, pair, lo = u % 3, u // 4, (P if u % 4 == 0 else 0)
                rows = bank[:, 2 * s:2 * s + 2, lo:256]
                mask = con("sw_mask", lo, 256 - lo).unsqueeze(1).to_broadcast([P, 2, 256 - lo])
                link(V.tensor_tensor(rows, rows, mask, ALU.add))
                link(V.tensor_reduce(stat_col(u, 8, 2), rows, AX.X, ALU.max))
                link(V.tensor_tensor(stat_col(u, 8, 2), stat_col(u, 8, 2), par("sinks", 2 * pair, 2), ALU.max))
                mark(V.tensor_scalar(stat_col(u, 0, 2), stat_col(u, 8, 2), -1.0, None, ALU.mult))
                V.tensor_tensor(stat_col(u, 4, 2), par("sinks", 2 * pair, 2), stat_col(u, 8, 2),
                                ALU.subtract).then_inc(asw["max"], 1)

            def sw_normalise(u):
                dve.wait_ge(asw["biased"], u + 1)
                link(V.tensor_tensor(stat_col(u, 10, 2), stat_col(u, 2, 2), stat_col(u, 6, 2), ALU.add))
                link(V.reciprocal(stat_col(u, 10, 2), stat_col(u, 10, 2)))
                lo = P if u % 4 == 0 else 0
                for e in range(2):
                    p = SQ5[:, u % 3, e * 256 + lo:(e + 1) * 256]
                    ins = V.tensor_scalar(p, p, stat_col(u, 10 + e), None, ALU.mult)
                    if e == 0:
                        mark(ins)
                ins.then_inc(asw["norm"], 1)

            attention(asw, 32, sw_maxima, sw_normalise, 4, lambda p: V.tensor_copy(QS[:, p, :], bank[:, 7, :]))

            link(V.tensor_copy(ROWS[0:4, 0:2, :], YA[0:4, 0:2, :]))
            link(V.tensor_scalar(ROWS[0:4, 5, :], ROWS[0:4, 1, :], -1.0, None, ALU.mult))
            V.tensor_tensor(ROWS[0:4, 5, :], ROWS[0:4, 5, :], ROWS[0:4, 1, :], ALU.max).then_inc(gate["lf"], 1)
            link(V.memset(YA[0:4, 2, :], 1.0))
            dve.wait_ge(gate["soft"], 1)
            link(V.scalar_tensor_tensor(ROWS[0:4, 1, :], ROWS[0:4, 1, :], 0.0, ROWS[0:4, 5, :], ALU.min, ALU.subtract))
            link(V.tensor_tensor_scan(ROWS[0:4, 5, :], YA[0:4, 2, :], ROWS[0:4, 1, :], 0.0, ALU.mult, ALU.add))
            link(V.tensor_tensor(ROWS[0:4, 2, :], ROWS[0:4, 0, :], ROWS[0:4, 5, :], ALU.subtract))
            link(V.tensor_tensor_scan(ROWS[0:4, 3, :], ROWS[0:4, 2, :], ROWS[0:4, 2, :], 0.0, ALU.max, ALU.max))
            V.tensor_tensor(ROWS[0:4, 4, :], ROWS[0:4, 3, :], ROWS[0:4, 5, :], ALU.add).then_inc(gate["rows"], 1)
            dve.wait_ge(gate["cols"], 1)
            V.tensor_copy(ACOL, bank[:, 7, 0:16].rearrange("p (c h) -> p c h", c=4)).then_inc(gate["ready"], 1)
            for h in range(X_HEADS):
                dve.wait_ge(ml["minus_m"], h + 1)
                for c in range(5):
                    if c < 4:
                        if c < 2 and h >= 1:
                            dve.wait_ge(ml["ssq"], h)
                        if c >= 2:
                            dve.wait_ge(ml["w"], 4 * h + c - 1)
                        V.tensor_tensor(SQ5[:, c % 2, 0:P], rs[:, c * P:(c + 1) * P], con("causal", 0, P),
                                        ALU.add).then_inc(ml["diag"], 1)
                    if c >= 1:
                        d = c - 1
                        dve.wait_ge(ml["e"], 4 * h + d + 1)
                        dve.wait_ge(ml["s"], 4 * h + d + 1)
                        if 4 * h + d >= 2:
                            dve.wait_ge(ml["used"], 4 * h + d - 1)
                        V.scalar_tensor_tensor(TMP5[:, d % 2, 0:S - d * P], bank[:, 2 + d % 2, 0:S - d * P],
                                               X_DK ** -0.5, SQ5[:, d % 2, 0:S - d * P], ALU.mult,
                                               ALU.mult).then_inc(ml["w"], 1)
                dve.wait_ge(ml["floor"], h + 1)
                dve.wait_ge(ml["acc"], h + 1)
                link(V.tensor_tensor(SQ5[:, 2, :], SQ5[:, 2, :], TMP5[:, 2, :], ALU.max))
                link(V.reciprocal(SQ5[:, 2, :], SQ5[:, 2, :]))
                mark(V.tensor_tensor(YA[:, 2 * h, :], bank[:, 4, :], SQ5[:, 2, :], ALU.mult))
                V.tensor_tensor(YA[:, 2 * h + 1, :], bank[:, 5, :], SQ5[:, 2, :], ALU.mult).then_inc(ml["num"], 1)
                dve.wait_ge(ml["root"], h + 1)
                link(V.reciprocal(rs[:, 0:S], rs[:, 0:S]))
                for v in range(2):
                    ins = V.scalar_tensor_tensor(YA[:, 2 * h + v, :], YA[:, 2 * h + v, :], par("mlstm_g", 2 * h + v),
                                                 rs[:, 0:S], ALU.mult, ALU.mult)
                    if v == 0:
                        mark(ins)
                ins.then_inc(ml["head"], 1)
            for b in range(8):
                dve.wait_ge(og["act"], b + 1)
                if b == 0:
                    dve.wait_ge(ml["head"], X_HEADS)
                V.tensor_tensor(YA[:, b, :], YA[:, b, :], TMP5[:, b % 2, :], ALU.mult).then_inc(og["free"], 1)
            merge(mrg2, MR2)
            residual_adds(nmlp, out2["done"])
            norm(nmlp, LAT, plain("mlp_g"), False)

            def up3_dve(i):
                for j in range(8):
                    dve.wait_ge(up3["act"], 8 * i + j + 1)
                    h = HID2[:, bass.ds(8 * i + j, 1), :].rearrange("p o t -> p (o t)")
                    V.scalar_tensor_tensor(h, bank[:, j % 4, :], 0.0, h, ALU.max, ALU.mult).then_inc(up3["free"], 1)
            rounds(dve, 0, FF2 // 8, up3_dve)
            residual_adds(nple, down3["done"])
            norm(nple, LAT, plain("ple_g"), False)
            for o in range(KC):
                s = o % 2
                dve.wait_ge(ple["gate"], o + 1)
                V.tensor_tensor(TMP5[:, s, :], TMP5[:, s, :], bank[:, 2 * s + 1, :], ALU.mult).then_inc(ple["free"], 1)
                dve.wait_ge(ple["free"], o + 1)
                V.tensor_tensor(X[:, o, 0:S], X[:, o, 0:S], TMP5[:, s, :], ALU.add).then_inc(nfin["xnew"], 1)
            norm(nfin, LAT, plain("final_g"), False)

        @block.gpsimd
        def _(pool):
            pool.wait_ge(inputs_landed, 16 * N_LOADS)
            pool.wait_ge(rpb_landed, 16)
            for u in range(NA_HEADS * N_BLK):
                h, j = u // N_BLK, u % N_BLK
                if u >= 2:
                    pool.wait_ge(ana["biased"], u - 1)
                at = K_START[j] - Q_COLS * j + Q_COLS
                nc.gpsimd.tensor_tensor(bm_t[:, 256 * (u % 2):256 * (u % 2) + 256].rearrange("p (a k) -> p a k", a=8),
                                        BIAS[:, h, :, at:at + K_COLS], con("na_mask", j * K_COLS, K_COLS).unsqueeze(1)
                                        .to_broadcast([P, GRID_H, K_COLS]), ALU.add).then_inc(ana["bias"], 1)


def _tiles(w, cols=P):
    k, n = w.shape
    return w.reshape(k // P, P, n // cols, cols).transpose(2, 1, 0, 3)


def _cols(v):
    return v.reshape(-1, P).T


def _weights(i):
    out = np.zeros((N_UNITS, P, UNIT), np.float32)

    def put(name, units):
        units = units.reshape(units.shape[0], P, -1)
        out[BASE[name]:BASE[name] + len(units), :, 0:units.shape[2]] = units

    def paired(w):
        t = _tiles(w).reshape(w.shape[1] // P, P, -1)
        return t.reshape(-1, 2, P, t.shape[2]).transpose(0, 2, 1, 3)

    ada = paired(i["w_ada"][0]).reshape(36, P, -1)
    put("ada_head", ada[:8])
    up = np.stack([_tiles(i["ffn1_w1"][0]), _tiles(i["ffn1_w3"][0])], 2).reshape(FF, P, -1)
    put("up1_ada", np.stack([up, ada[8:8 + FF]], 1).reshape(2 * FF, P, -1))
    put("ada_tail", ada[8 + FF:])

    def down(w):
        return _tiles(w).reshape(KC, P, 2, -1).transpose(0, 2, 1, 3).reshape(2 * KC, P, -1)

    put("down1", down(i["ffn1_w2"][0]))
    w_in = i["w_in"][0]
    put("proj", paired(w_in[:, 0:2560]))
    put("kr", _tiles(np.concatenate([np.zeros((D, NOPE), np.float32), w_in[:, 2560:2592]], 1), QK_D))
    uq = _tiles(i["w_uq"][0], QK_D)
    put("uq", uq.reshape(4, 2, P, -1).transpose(0, 2, 1, 3))
    ukv = i["w_ukv"][0].reshape(ML_KV_RANK, NA_HEADS, 2, 64)
    put("ukv_k", _tiles(ukv[:, :, 0].reshape(ML_KV_RANK, 512), 64).transpose(1, 0, 2, 3)[None])
    put("ukv_v", _tiles(ukv[:, :, 1].reshape(ML_KV_RANK, 512), 512))
    gates = _tiles(w_in[:, 2592:])

    def with_branches(g, a, b):
        both = [np.concatenate([g[q * KC:(q + 1) * KC], _tiles(w)], 2) for q, w in ((0, a), (1, b))]
        return np.stack(both, 1).reshape(2 * KC, P, -1)

    put("merge1", with_branches(gates, i["w_o_na"][0], i["w_o_mla"][0]))
    put("out1", paired(i["w_out"][0]))
    put("up2", np.stack([_tiles(i["ffn2_w1"][0]), _tiles(i["ffn2_w3"][0])], 2).reshape(FF, P, -1))
    put("down2", down(i["ffn2_w2"][0]))
    w2 = i["w_in_2"][0]
    put("qk_m", paired(w2[:, 0:1024]))
    put("v_m", _tiles(w2[:, 1024:2048], 256))
    put("o_m", paired(w2[:, 2048:3072]))
    between = np.zeros((D, 28), np.float32)
    put("if_m", _tiles(np.concatenate([w2[:, 3072:3076], between, w2[:, 3076:3080]], 1), 36))
    put("q_sw", paired(w2[:, 3080:4104]))
    put("k_sw", paired(w2[:, 4104:4360]))
    put("v_sw", _tiles(w2[:, 4360:4616], 256))
    put("merge2", with_branches(_tiles(w2[:, 4616:]), i["w_branch_a_2"][0], i["w_branch_b_2"][0]))
    put("out2", paired(i["w_out_2"][0]))
    put("up3", paired(i["w_up_2"][0]))
    put("down3", down(i["w_down_2"][0]))
    put("ple", np.concatenate([_tiles(i["w_ple_gate_2"][0]), _tiles(i["w_ple_proj_2"][0])], 2).reshape(KC, P, -1))
    return out


def _params(i):
    p = np.zeros((P, N_PARAM), np.float32)

    def put(name, a):
        p[0:a.shape[0], PARAM[name]:PARAM[name] + a.shape[1]] = a

    put("b_ada", np.repeat(_cols(i["b_ada"][0]), 2, axis=1))
    put("norm_g", np.repeat(_cols(i["norm_g"][0].reshape(-1)), 2, axis=1))
    put("b_gate", _cols(i["b_gate"][0]))
    put("g_q", _cols(i["g_q_lora"][0]))
    put("g_kv", _cols(i["g_kv_lora"][0]))
    put("mix_g", _cols(i["norm_mix_g_2"][0]))
    put("mlstm_g", _cols(i["mlstm_norm_g_2"][0]))
    put("mlp_g", _cols(i["norm_mlp_g_2"][0]))
    put("ple_g", _cols(i["norm_ple_g_2"][0]))
    put("final_g", _cols(i["final_norm_g_2"]))
    put("conv", i["conv_qk_2"][0].reshape(4, KC, P).transpose(2, 1, 0).reshape(P, -1))
    put("sinks", np.repeat(i["sinks_2"], P, axis=0))
    p[0:4, PARAM["b_if"]] = i["b_if_2"][0, 0:4]
    p[32:36, PARAM["b_if"] + 1] = i["b_if_2"][0, 4:8]
    put("eps", np.full((P, 1), EPS, np.float32))
    return p


def _consts():
    c = np.zeros((P, N_CONST), np.float32)

    def put(name, a):
        c[0:a.shape[0], CONST[name]:CONST[name] + a.shape[1]] = a

    put("ident", np.eye(P))
    put("ones", np.ones((P, P)))
    half = ROPE // 4
    rot = np.zeros((QK_D, QK_D))
    freqs = (10000.0 ** (-np.arange(half, dtype=np.float32) / half)).astype(np.float32)
    tok = np.arange(S)
    cos, sin = np.ones((QK_D, S), np.float32), np.zeros((QK_D, S), np.float32)
    for axis, pos in ((0, tok // GRID_W), (1, tok % GRID_W)):
        at = NOPE + axis * 2 * half
        ang = freqs[:, None] * pos[None, :].astype(np.float32)
        for side in range(2):
            cos[at + side * half:at + (side + 1) * half] = np.cos(ang)
            sin[at + side * half:at + (side + 1) * half] = np.sin(ang)
        for r in range(half):
            rot[at + half + r, at + r] = -1.0
            rot[at + r, at + half + r] = 1.0
    put("rot", rot)
    put("cos", cos)
    put("sin", sin)
    put("select", np.kron(np.eye(4), np.ones((1, P))))
    q, k = np.arange(P)[:, None] % Q_COLS, np.arange(K_COLS)[None, :]
    na = []
    for j in range(N_BLK):
        start = np.clip(j * Q_COLS + q - WIN_W // 2, 0, GRID_W - WIN_W)
        col = K_START[j] + k
        na.append(np.where((col >= start) & (col < start + WIN_W), 0.0, NEG))
    put("na_mask", np.concatenate(na, 1))
    diff = np.arange(P)[:, None] + SW_W - np.arange(2 * P)[None, :]
    put("sw_mask", np.where((diff >= 0) & (diff < SW_W), 0.0, NEG))
    put("causal", np.where(np.arange(P)[None, :] >= np.arange(P)[:, None], 0.0, NEG))
    return c


def _rpb_rows(rpb):
    pad = np.pad(rpb, ((0, 0), (0, 0), (Q_COLS, Q_COLS + 1)))
    out = np.zeros((GRID_H, Q_COLS, NA_HEADS, GRID_H, BIAS_W), np.float32)
    for r in range(GRID_H):
        for c in range(Q_COLS):
            at = WIN_W - 1 - c
            out[r, c] = pad[:, GRID_H - 1 - r:2 * GRID_H - 1 - r, at:at + BIAS_W]
    return out.reshape(P, -1)


def kernel(**inputs):
    import concourse.bacc as _bacc
    from concourse.bass_utils import run_bass_kernel_spmd as _run

    i = {k: np.asarray(v) for k, v in inputs.items()}
    nc = _bacc.Bacc("TRN2", target_bir_lowering=False, num_devices=1)
    tokens = np.concatenate([i["x"][0], i["ctx"][0]], 0)
    arrays = {
        "xT": np.ascontiguousarray(tokens.T.reshape(KC, P, T).transpose(1, 0, 2)),
        "cT": np.ascontiguousarray(np.stack([_cols(i["c"][0]), _cols(i["c_ctx"])], 2)),
        "params": _params(i),
        "consts": _consts(),
        "weights": _weights(i),
        "rpb": _rpb_rows(i["rpb"][0]),
        "pT": np.ascontiguousarray(i["p_2"][0, 0].T.reshape(2, P, S).transpose(1, 0, 2)),
    }
    aps = {n: nc.dram_tensor(n, a.shape, F32, kind="ExternalInput").ap() for n, a in arrays.items()}
    out = nc.dram_tensor("out", (D, S), F32, kind="ExternalOutput").ap()
    build(nc, aps["xT"], aps["cT"], aps["params"], aps["consts"], aps["weights"], aps["rpb"], aps["pT"], out)
    r = _run(nc, [arrays], core_ids=[0])
    return np.ascontiguousarray(r.results[0]["out"].T)[None]
```

```python
from contextlib import ExitStack

import numpy as np

import concourse.bass as bass
from concourse import mybir

F32 = mybir.dt.float32
ALU = mybir.AluOpType
ACT = mybir.ActivationFunctionType
AX = mybir.AxisListType

P = 128
D = 1024
KC = D // P
S = 512
CTX = 256
T = S + CTX
EPS = 1e-6
NEG = -1e30
N_MOD = 9
GRID_W, GRID_H = 64, 8
N_BLK, Q_COLS, K_COLS, WIN_W = 4, 16, 32, 16
K_START = [min(max(j * Q_COLS - WIN_W // 2, 0), GRID_W - K_COLS) for j in range(N_BLK)]
NA_HEADS, NA_D = 8, 64
ML_Q_RANK, ML_KV_RANK, NOPE, ROPE, V_D = 768, 256, 64, 32, 64
QK_D = NOPE + ROPE
QR, KVR = ML_Q_RANK // P, ML_KV_RANK // P
FF = 2816 // P
FF2 = 4 * D // P
RPB_H, RPB_W = 15, 31
BIAS_W = K_COLS + Q_COLS
X_HEADS, X_DK, X_DV = 4, 128, 256
SW_HEADS, SW_KV, SW_D, SW_W = 16, 4, 64, 128

RING = 4
UNIT = 16 * P
UNITS = [
    ("up1", FF, UNIT), ("down1", 16, 11 * P),
    ("proj", 10, UNIT), ("kr", 1, KC * QK_D), ("uq", 4, 2 * QR * QK_D), ("ukv_k", 1, NA_HEADS * KVR * NOPE),
    ("ukv_v", 1, KVR * 512), ("merge1", 16, 12 * P), ("out1", 4, UNIT), ("up2", FF, UNIT), ("down2", 16, 11 * P),
    ("qk_m", 4, UNIT), ("v_m", 4, UNIT), ("q_sw", 4, UNIT), ("k_sw", 1, UNIT), ("v_sw", 1, UNIT),
    ("if_m", 1, KC * 36), ("o_m", 4, UNIT), ("merge2", 16, UNIT), ("out2", 4, UNIT), ("up3", 16, UNIT),
    ("down3", 16, UNIT), ("ple", 8, 10 * P),
]
BASE, _n = {}, 0
for _name, _count, _floats in UNITS:
    BASE[_name] = _n
    _n += _count
N_UNITS = _n


def _places(columns):
    at, out = 0, {}
    for name, n in columns:
        out[name] = at
        at += n
    return out, at


PARAM, N_PARAM = _places([("b_ada", 2 * N_MOD * KC), ("norm_g", 2 * 6 * KC), ("b_gate", 2 * KC), ("g_q", QR),
                          ("g_kv", KVR), ("mix_g", KC), ("mlstm_g", KC), ("mlp_g", KC), ("ple_g", KC),
                          ("final_g", KC), ("conv", 4 * KC), ("sinks", SW_HEADS), ("b_if", 2), ("eps", 1)])
CONST, N_CONST = _places([("ident", P), ("ones", P), ("rot", QK_D), ("cos", S), ("sin", S), ("select", 4 * P),
                          ("na_mask", N_BLK * K_COLS), ("sw_mask", 2 * P), ("causal", P)])
LAT = [(0, S, 0)]
BOTH = [(0, S, 0), (S, T, 1)]
NA_S = (0, 1, 6)
SCALE1, SCALE2, SCALE3, GATE1, GATE2, GATE3 = range(6)


OG_IN = ((2,), (3, 4), (5,), (6, 7))


def build(nc, xT, cB, w_ada, params, consts, weights, rpb, pT, out):
    with ExitStack() as ctx:
        def sb(name, n):
            return ctx.enter_context(nc.sbuf_tensor(name, [P, n], F32))

        def sem(name):
            return ctx.enter_context(nc.semaphore(name))

        def view(t, at, a, b):
            return t[:, at:at + a * b].rearrange("p (a b) -> p a b", a=a)

        bank = ctx.enter_context(nc.psum_tensor("banks", [P, 8, 512], F32))
        x_t = sb("residual", KC * T)
        h_t = sb("normed", KC * T)
        big = sb("big", 20736)
        ring = sb("weight_ring", RING * UNIT)
        sq_t = sb("scratch_a", 2 * T)
        tmp_t = sb("scratch_b", 2 * T)
        rs = sb("rstd", T)
        prm = sb("params_sb", N_PARAM)
        cst = sb("consts_sb", N_CONST)
        bias_t = sb("rpb_rows", NA_HEADS * GRID_H * BIAS_W)
        BIAS = bias_t[:, :].rearrange("p (h a w) -> p h a w", h=NA_HEADS, a=GRID_H)
        mods_t = sb("mods", 2 * N_MOD * KC)
        coef_t = sb("coefs", 6 * KC * 2)
        ada_acc = sb("ada_acc", 8)
        stat = sb("stat", 64)
        bm_t = sb("bias_mask", 2 * 256)
        p_sb = sb("p_embed", 2 * S)

        X = view(x_t, 0, KC, T)
        H = view(h_t, 0, KC, T)
        SQ = view(sq_t, 0, 2, T)
        TMP = view(tmp_t, 0, 2, T)
        SQ5 = view(sq_t, 0, 3, S)
        TMP5 = view(tmp_t, 0, 3, S)
        MODS = mods_t[:, :].rearrange("p (m c) -> p m c", c=2)
        COEF = coef_t[:, :].rearrange("p (g k c) -> p g k c", g=6, c=2)
        PE2 = view(p_sb, 0, 2, S)
        CS = view(bias_t, 0, 2, D)
        ADA_HEAD = view(big, 0, 2 * KC, D)
        ADA_PAIR = [[view(big, FF * T, 3, D)[:, q, :] for q in range(2)],
                    [view(big, FF * T, 3, D)[:, 2, :], bias_t[:, 2 * D:3 * D]]]

        def par(name, i=0, n=1, rows=P):
            return prm[0:rows, PARAM[name] + i:PARAM[name] + i + n]

        def con(name, i, n, rows=P):
            return cst[0:rows, CONST[name] + i:CONST[name] + i + n]

        ident, ones = con("ident", 0, P), con("ones", 0, P)
        eps = par("eps")

        HID = view(big, 0, FF, T)
        QA = view(big, 0, 4, S)
        KA = view(big, 2048, 4, T)
        VA = view(big, 5120, 4, N_BLK * 256 + CTX)
        CQ = view(big, 10240, QR, S)
        CKV = view(big, 13312, KVR, T)
        KR = big[:, 14848:14848 + T]
        VN = view(big, 15616, 10, 512)
        KM = view(big, 2048, NA_HEADS, T)
        OM = view(big, 8192, 4, S)
        QM = view(big, 15616, NA_HEADS, S)
        VM = view(big, 10240, 6, 512)
        PM = view(big, 13312, 3, T)
        MR1 = view(big, 2048, KC, S)
        HID2 = view(big, 0, FF2, S)
        QK = view(big, 0, 8, S)
        VX = view(big, 4096, 4, 1024)
        QS = view(big, 8192, 8, S)
        KS = view(big, 12288, SW_KV, S)
        VS = view(big, 14336, 4, 256)
        YA = view(big, 15360, 8, S)
        MR2 = view(big, 0, KC, S)
        OG = [view(bias_t, 0, 6, S)[:, b, :] if b < 6 else PE2[:, b - 6, :] for b in range(8)]
        ROWS = view(big, 12288, 6, S)
        ACOL = big[:, 19456:19456 + 16].rearrange("p (c h) -> p c h", c=4)

        landed = [sem(f"weights_landed_{i}") for i in range(RING)]
        unit_begun = sem("unit_begun")
        inputs_landed, rpb_landed, stored = sem("inputs_landed"), sem("rpb_landed"), sem("output_stored")
        N_LOADS = 4
        dve_c = sem("dve_chain")

        def stages(count, name, *signals):
            shared = {s: sem(f"{name}_{s}") for s in signals}
            return [dict(shared, base=i * KC, turn=i) for i in range(count)]

        def st(name, *signals):
            return stages(1, name, *signals)[0]

        ada = st("ada", "c_landed", "silu", "landed0", "landed1", "landed2", "landed3", "pair_landed0",
                 "pair_landed1", "done", "got")
        p_landed = sem("p_landed")
        up1, up2, up3 = (st(f"up{i}", "done", "act", "free") for i in (1, 2, 3))
        down1, out1, down2 = stages(3, "sublayer", "done", "free", "sq", "sq_used")
        out2, down3 = stages(2, "add", "done")
        n0 = st("norm_0", "sq", "sq_used", "root", "scaled", "ready")
        na, nb = (st(f"norm_{n}", "y_root", "xnew", "sq", "sq_used", "root", "scaled", "ready") for n in ("a", "b"))
        nmix = st("norm_mix", "y_root", "xnew", "sq", "sq_used", "root", "ready")
        nmlp, nple, nfin = stages(3, "norm_late", "xnew", "sq", "sq_used", "root", "ready")
        proj = st("proj", "done", "act", "dve")
        vt = st("vt", "done", "act", "dve")
        ana = st("att_na", "s", "bias", "biased", "max", "exp", "norm", "t", "tc", "pv", "oc")
        amla = st("att_mla", "s", "max", "exp", "norm", "t", "tc", "pv", "oc")
        asw = st("att_sw", "s", "biased", "max", "exp", "norm", "t", "tc", "pv", "oc")
        lora = st("lora", "sq", "sq_used", "root", "normed")
        gen = st("mla_gen", "kr", "kr_roped", "q", "qc", "rot", "q_roped", "k", "kc", "v", "vc")
        mrg1, mrg2 = stages(2, "merge", "done", "gate", "free")
        ple = st("ple", "done", "gate", "free")
        conv = st("conv", "raw", "mixed", "ready")
        prj2 = st("proj2", "done", "act", "dve")
        gate = st("gates", "pre", "exp", "lf", "soft", "rows", "cols", "ready")
        ml = st("mlstm", "bcast", "minus_m", "diag", "e", "s", "w", "used", "acc", "floor", "num", "sq", "ssq", "root", "head")
        og = st("ogate", "done", "act", "gate", "free")

        block = ctx.enter_context(nc.Block())

        def grid_cols(rows, first):
            return rows.rearrange("p (r w) -> p r w", w=GRID_W)[:, :, first:first + K_COLS]

        def q_blocks(b):
            dst = QA[:, b, :].rearrange("p (j r c) -> p r j c", j=N_BLK, r=GRID_H)
            return dst, bank[:, 2 * (b % 3), :].rearrange("p (r j c) -> p r j c", r=GRID_H, j=N_BLK)

        def v_blocks(b):
            s = b % 3
            pairs = [(VA[:, b - 8, j * 256:(j + 1) * 256].rearrange("p (r w) -> p r w", w=K_COLS),
                      grid_cols(bank[:, 2 * s, :], K_START[j])) for j in range(N_BLK)]
            return pairs + [(VA[:, b - 8, N_BLK * 256:], bank[:, 2 * s + 1, 0:CTX])]

        def slot(n, at=0, k=UNIT):
            base = (n % RING) * UNIT + at
            return ring[:, base:base + k]

        def rounds(eng, lo, hi, body):
            with eng.Fori(lo, hi) as i:
                body(i)

        @block.sync
        def _(sp):
            def load(n, i, floats):
                if n + (0 if isinstance(i, int) else RING) >= RING:
                    sp.wait_ge(unit_begun, i * RING + (n - RING + 2))
                src = weights[n + RING * i] if isinstance(i, int) else \
                    weights[bass.ds(i * RING + n, 1)].rearrange("o p f -> p (o f)")
                sp.dma_start(slot(n, 0, floats), src[:, 0:floats]).then_inc(landed[n % RING], 16)

            sp.wait_ge(ada["landed2"], 16)
            for name, count, floats in UNITS:
                n, whole = BASE[name], 0
                if count // RING >= 2:
                    whole = count // RING
                    first = 1 if n < RING else 0
                    for j in range(RING * first):
                        load(n + j, 0, floats)

                    def body(i):
                        for j in range(RING):
                            load(n + j, i, floats)
                    rounds(sp, first, whole, body)
                for j in range(whole * RING, count):
                    load(n + j, 0, floats)
            for k in range(0, KC, 2):
                sp.wait_ge(nfin["ready"], 2 * KC + k + 2)
                sp.dma_start(out.rearrange("(k p) t -> p k t", p=P)[:, k:k + 2, :],
                             H[:, k:k + 2, 0:S]).then_inc(stored, 16)
            sp.wait_ge(stored, 16 * KC // 2)

        @block.tensor
        def _(pe):
            def begin(n, i=0):
                pe.wait_ge(landed[n % RING], i * 16 + 16 * (n // RING + 1))

            def mm(o, w, r, start, stop, first=False):
                ins = nc.tensor.matmul(o, w, r, start=start, stop=stop)
                if first:
                    ins.then_inc(unit_begun, 1)
                return ins

            def sum_squares(g, k, parts, banks, count=KC):
                pe.wait_ge(g["sq"], g["base"] + k + 1)
                for (a, b, _), n in zip(parts, banks):
                    last = nc.tensor.matmul(bank[:, n, 0:b - a], ones, SQ[:, k % 2, a:b],
                                            start=(k == 0), stop=(k == count - 1))
                return last

            def norm_sums(g, parts):
                for k in range(KC):
                    sum_squares(g, k, parts, (6, 5)).then_inc(g["sq_used"], 1)

            def swiglu_up(g, n, i, s, parts, ready, first):
                begin(n, i)
                for w in range(2):
                    for k in range(KC):
                        if first and w == 0:
                            pe.wait_ge(ready, len(parts) * (k + 1))
                        for a, b, c in parts:
                            o = bank[:, 3 * s + w, 0:S] if c == 0 else bank[:, 3 * s + 2, w * CTX:(w + 1) * CTX]
                            last = mm(o, slot(n, (w * KC + k) * P, P), H[:, k, a:b], k == 0, k == KC - 1,
                                      w == 0 and k == 0 and c == 0)
                last.then_inc(g["done"], 1)

            def out_chunks(g, free, n, i, o0, tiles, rhs, parts, per_unit, sums=None, peel=False):
                unit = -1
                for j in range(2):
                    if not (peel):
                        pe.wait_ge(free, o0 + (g["base"] + j - 1))
                    for t in range(tiles):
                        at = j * tiles + t
                        new = at // per_unit != unit
                        unit = at // per_unit
                        if new:
                            begin(n + unit, i)
                        for a, b, c in parts:
                            last = mm(bank[:, 2 * j + c, 0:b - a], slot(n + unit, (at % per_unit) * P, P),
                                      rhs[:, t, a:b], t == 0, t == tiles - 1, new and c == 0)
                    last.then_inc(g["done"], 1)
                    if sums and not (peel and j == 0):
                        sg, banks = sums
                        pe.wait_ge(sg["sq"], o0 + (sg["base"] + j))
                        for (a, b, _), q in zip(parts, banks):
                            last = nc.tensor.matmul(bank[:, q, 0:b - a], ones, SQ[:, 1 - j, a:b],
                                                    start=(peel and j == 1), stop=False)
                        last.then_inc(sg["sq_used"], 1)

            def out_projection(g, free, name, tiles, rhs, parts, per_unit, sums):
                units = 2 * tiles // per_unit
                out_chunks(g, free, BASE[name], 0, 0, tiles, rhs, parts, per_unit, sums, peel=True)
                if units == RING:
                    rounds(pe, 1, KC // 2, lambda i: out_chunks(g, free, BASE[name], i, 2 * i, tiles, rhs, parts,
                                                                per_unit, sums))
                else:
                    for i in range(1, KC // 2):
                        out_chunks(g, free, BASE[name] + units * i, 0, 2 * i, tiles, rhs, parts, per_unit, sums)
                sg, banks = sums
                sum_squares(sg, KC - 1, parts, banks).then_inc(sg["sq_used"], 1)

            def merged(g, name, per_branch, branch_a, branch_b, rows_ready=None):
                for o in range(KC):
                    s = o % 2
                    if o >= 2:
                        pe.wait_ge(g["free"], g["base"] + o - 1)
                    for q, rows in ((0, branch_a), (1, branch_b)):
                        n = BASE[name] + 2 * o + q
                        begin(n)
                        for k in range(KC):
                            mm(bank[:, 4 * s + q, :], slot(n, k * P, P), H[:, k, 0:S], k == 0, k == KC - 1, k == 0)
                        for k in range(per_branch):
                            if rows_ready is not None and o == 0 and q == 0:
                                pe.wait_ge(rows_ready, k + 1)
                            last = mm(bank[:, 4 * s + 2 + q, :], slot(n, (KC + k) * P, P), rows[:, k, :],
                                      k == 0, k == per_branch - 1)
                    last.then_inc(g["done"], 1)

            def attention(g, units, exps, scores, pieces, values, s_sets, t_banks, o_banks, per_out):
                turned = 0
                upto = [0]
                for u in range(units):
                    upto.append(upto[-1] + len(pieces(u)))
                for i in range(units + 3):
                    if i < units:
                        if i >= s_sets:
                            pe.wait_ge(g["exp"], exps * (i - s_sets + 1))
                        scores(i).then_inc(g["s"], 1)
                    if 2 <= i < units + 2:
                        u = i - 2
                        pe.wait_ge(g["norm"], u + 1)
                        for piece in pieces(u):
                            if turned >= len(t_banks):
                                pe.wait_ge(g["tc"], turned - len(t_banks) + 1)
                            for c, source in enumerate(piece):
                                last = nc.tensor.transpose(
                                    bank[:, t_banks[turned % len(t_banks)], c * P:(c + 1) * P], source, ident)
                            last.then_inc(g["t"], 1)
                            turned += 1
                    if i >= 3:
                        u = i - 3
                        pe.wait_ge(g["tc"], upto[u + 1])
                        if u % per_out == 0 and u // per_out >= o_banks:
                            pe.wait_ge(g["oc"], u // per_out - o_banks + 1)
                        values(u).then_inc(g["pv"], 1)

            def up_rounds(g, name, parts, ready):
                def body(i, first=False, count=RING, f0=0):
                    for j in range(count):
                        if not (first and j < 2):
                            pe.wait_ge(g["free"], RING * i + (f0 + j - 1))
                        swiglu_up(g, BASE[name] + f0 + j, i, j % 2, parts, ready, first and j == 0)
                body(0, first=True)
                rounds(pe, 1, FF // RING, body)
                body(0, count=FF % RING, f0=FF // RING * RING)
                pe.wait_ge(g["free"], FF)

            pe.wait_ge(inputs_landed, 16 * N_LOADS)
            norm_sums(n0, BOTH)
            up_rounds(up1, "up1", BOTH, n0["ready"])
            out_projection(down1, down1["free"], "down1", FF, HID, BOTH, 11, (down1, (4, 5)))
            norm_sums(na, BOTH)

            for b in range(21):
                n = BASE["proj"] + b // 2
                s = b % 3
                parts = LAT if b < 4 or 12 <= b < 18 else BOTH
                if b % 2 == 0:
                    begin(n)
                if b >= 3:
                    pe.wait_ge(proj["dve"] if (b - 3) % 2 else proj["act"], (b - 3) // 2 + 1)
                m = QK_D if b == 20 else P
                for k in range(KC):
                    if b == 0:
                        pe.wait_ge(na["ready"], 2 * (k + 1))
                    w = slot(n, ((b % 2) * KC + k) * P, P) if b < 20 else slot(n, k * QK_D, QK_D)
                    for x, y, c in parts:
                        last = mm(bank[0:m, 2 * s + c, 0:y - x], w, H[:, k, x:y], k == 0, k == KC - 1,
                                  b % 2 == 0 and k == 0 and c == 0)
                last.then_inc(proj["done"], 1)

            pe.wait_ge(proj["act"], 11)
            pe.wait_ge(proj["dve"], 10)
            for v in range(10):
                if v >= 4:
                    pe.wait_ge(vt["dve"] if v % 2 else vt["act"], (v - 4) // 2 + 1)
                for c in range(4):
                    last = nc.tensor.transpose(bank[:, v % 4, c * P:(c + 1) * P], VA[:, c, v * P:(v + 1) * P], ident)
                last.then_inc(vt["done"], 1)
            pe.wait_ge(vt["act"], 5)
            pe.wait_ge(vt["dve"], 5)

            def na_scores(u):
                h, j = u // N_BLK, u % N_BLK
                e = NA_D * (h % 2)
                q = QA[e:e + NA_D, h // 2, j * P:(j + 1) * P]
                nc.tensor.matmul(bank[:, NA_S[u % 3], 0:256].rearrange("p (r w) -> p r w", w=K_COLS), q,
                                 grid_cols(KA[e:e + NA_D, h // 2, 0:S], K_START[j]), start=True, stop=True)
                return nc.tensor.matmul(bank[:, NA_S[u % 3], 256:512], q, KA[e:e + NA_D, h // 2, S:T],
                                        start=True, stop=True)

            def na_values(u):
                h, j = u // N_BLK, u % N_BLK
                e = NA_D * (h % 2)
                for c in range(4):
                    v = VN[:, 2 * j + c if c < 2 else 6 + c, NA_D * h:NA_D * (h + 1)]
                    last = nc.tensor.matmul(bank[e:e + NA_D, 4 + h % 2, j * P:(j + 1) * P], v,
                                            TMP[:, u % 2, c * P:(c + 1) * P], start=(c == 0), stop=(c == 3))
                return last

            attention(ana, NA_HEADS * N_BLK, 1, na_scores,
                      lambda u: [[SQ5[:, u % 3, c * P:(c + 1) * P] for c in range(4)]], na_values, 3, (2, 3), 2, N_BLK)

            for k in range(QR):
                pe.wait_ge(lora["sq"], k + 1)
                if k == 0:
                    pe.wait_ge(ana["oc"], NA_HEADS)
                nc.tensor.matmul(bank[:, 0, :], ones, SQ[:, k % 2, 0:S], start=(k == 0),
                                 stop=(k == QR - 1)).then_inc(lora["sq_used"], 1)
            for k in range(KVR):
                pe.wait_ge(lora["sq"], QR + k + 1)
                nc.tensor.matmul(bank[:, 1, :], ones, SQ[:, k % 2, 0:S], start=(k == 0), stop=(k == KVR - 1))
                nc.tensor.matmul(bank[:, 2, 0:CTX], ones, SQ[:, k % 2, S:T], start=(k == 0),
                                 stop=(k == KVR - 1)).then_inc(lora["sq_used"], 1)
            nc.tensor.matmul(bank[0:QK_D, 3, :], con("rot", 0, QK_D, QK_D), KR[0:QK_D, 0:S], start=True,
                             stop=True).then_inc(gen["kr"], 1)
            for h in range(NA_HEADS):
                n = BASE["uq"] + h // 2
                if h % 2 == 0:
                    begin(n)
                if h >= 2:
                    pe.wait_ge(gen["qc"], h - 1)
                for k in range(QR):
                    if h == 0:
                        pe.wait_ge(lora["normed"], k + 1)
                    last = mm(bank[0:QK_D, 4 + h % 2, :], slot(n, ((h % 2) * QR + k) * QK_D, QK_D), CQ[:, k, :],
                              k == 0, k == QR - 1, h % 2 == 0 and k == 0)
                last.then_inc(gen["q"], 1)
                if h >= 1:
                    if h >= 3:
                        pe.wait_ge(gen["q_roped"], h - 2)
                    pe.wait_ge(gen["qc"], h)
                    nc.tensor.matmul(bank[0:QK_D, 6 + (h - 1) % 2, :], con("rot", 0, QK_D, QK_D),
                                     QM[0:QK_D, h - 1, :], start=True, stop=True).then_inc(gen["rot"], 1)
            pe.wait_ge(gen["q_roped"], NA_HEADS - 2)
            pe.wait_ge(gen["qc"], NA_HEADS)
            nc.tensor.matmul(bank[0:QK_D, 7, :], con("rot", 0, QK_D, QK_D), QM[0:QK_D, 7, :], start=True,
                             stop=True).then_inc(gen["rot"], 1)
            n = BASE["ukv_k"]
            begin(n)
            pe.wait_ge(gen["kr_roped"], 1)
            for h in range(NA_HEADS):
                if h >= 2:
                    pe.wait_ge(gen["kc"], h - 1)
                for k in range(KVR):
                    w = slot(n, (h * KVR + k) * NOPE, NOPE)
                    mm(bank[0:NOPE, 2 * (h % 2), :], w, CKV[:, k, 0:S], k == 0, k == KVR - 1, h == 0 and k == 0)
                for k in range(KVR):
                    last = mm(bank[0:NOPE, 2 * (h % 2) + 1, 0:CTX], slot(n, (h * KVR + k) * NOPE, NOPE),
                              CKV[:, k, S:T], k == 0, k == KVR - 1)
                last.then_inc(gen["k"], 1)
            n = BASE["ukv_v"]
            begin(n)
            for t in range(6):
                if t >= 2:
                    pe.wait_ge(gen["vc"], t - 1)
                for k in range(KVR):
                    last = mm(bank[:, 4 + t % 2, :], CKV[:, k, t * P:(t + 1) * P], slot(n, k * 512, 512),
                              k == 0, k == KVR - 1, t == 0 and k == 0)
                last.then_inc(gen["v"], 1)
            pe.wait_ge(gen["kc"], NA_HEADS)
            pe.wait_ge(gen["vc"], 6)
            pe.wait_ge(gen["q_roped"], NA_HEADS)

            def mla_scores(u):
                h, b = u // 4, u % 4
                q = QM[0:QK_D, h, b * P:(b + 1) * P]
                nc.tensor.matmul(bank[:, 2 * (u % 2), :], q, KM[0:QK_D, h, 0:S], start=True, stop=True)
                return nc.tensor.matmul(bank[:, 2 * (u % 2) + 1, 0:CTX], q, KM[0:QK_D, h, S:T], start=True, stop=True)

            def mla_values(u):
                h, b = u // 4, u % 4
                e = V_D * (h % 2)
                for c in range(6):
                    last = nc.tensor.matmul(bank[e:e + V_D, 6 + h % 2, b * P:(b + 1) * P],
                                            VM[:, c, V_D * h:V_D * (h + 1)], TMP[:, u % 2, c * P:(c + 1) * P],
                                            start=(c == 0), stop=(c == 5))
                return last

            attention(amla, NA_HEADS * 4, 1, mla_scores,
                      lambda u: [[PM[:, u % 3, c * P:(c + 1) * P] for c in r] for r in (range(3), range(3, 6))],
                      mla_values, 2, (4, 5), 2, 4)

            pe.wait_ge(amla["oc"], NA_HEADS)
            merged(mrg1, "merge1", 4, QA, OM)
            pe.wait_ge(mrg1["free"], KC)
            out_projection(out1, out1["free"], "out1", KC, MR1, LAT, 16, (out1, (4, 5)))
            norm_sums(nb, LAT)

            up_rounds(up2, "up2", LAT, nb["ready"])
            out_projection(down2, down2["free"], "down2", FF, HID, LAT, 11, (down2, (4, 5)))
            norm_sums(nmix, LAT)

            for b in range(8):
                n = BASE["qk_m"] + b // 2
                if b % 2 == 0:
                    begin(n)
                if b >= 4:
                    pe.wait_ge(conv["mixed"], b - 3)
                for k in range(KC):
                    if b == 0:
                        pe.wait_ge(nmix["ready"], k + 1)
                    last = mm(bank[:, b % 4, :], slot(n, ((b % 2) * KC + k) * P, P), H[:, k, 0:S], k == 0,
                              k == KC - 1, b % 2 == 0 and k == 0)
                last.then_inc(conv["raw"], 1)
            pe.wait_ge(conv["mixed"], 8)
            for b in range(20):
                if b >= 4:
                    pe.wait_ge(prj2["dve"] if b % 2 else prj2["act"], (b - 4) // 2 + 1)
                n = BASE["v_m"] + b // 2
                if b % 2 == 0:
                    begin(n)
                if b < 8 or b >= 18:
                    for q in range(2):
                        tt = 2 * (b % 2) + q
                        for k in range(KC):
                            last = mm(bank[:, b % 4, q * 256:(q + 1) * 256], H[:, k, tt * P:(tt + 1) * P],
                                      slot(n, k * 256, 256), k == 0, k == KC - 1, b % 2 == 0 and q == 0 and k == 0)
                else:
                    for k in range(KC):
                        last = mm(bank[:, b % 4, :], slot(n, ((b % 2) * KC + k) * P, P), H[:, k, 0:S], k == 0,
                                  k == KC - 1, b % 2 == 0 and k == 0)
                last.then_inc(prj2["done"], 1)
            n = BASE["if_m"]
            begin(n)
            for k in range(KC):
                last = mm(bank[0:36, 6, :], slot(n, k * 36, 36), H[:, k, 0:S], k == 0, k == KC - 1, k == 0)
            last.then_inc(gate["pre"], 1)
            pe.wait_ge(prj2["act"], 10)
            pe.wait_ge(prj2["dve"], 10)

            def sw_scores(u):
                pair, blk = u // 4, u % 4
                lo = max(blk - 1, 0) * P
                for e in range(2):
                    last = nc.tensor.matmul(bank[:, 2 * (u % 2) + e, (P if blk == 0 else 0):2 * P],
                                            QS[64 * e:64 * e + 64, pair, blk * P:(blk + 1) * P],
                                            KS[64 * e:64 * e + 64, pair // 2, lo:(blk + 1) * P],
                                            start=True, stop=True)
                return last

            def sw_pieces(u):
                blk = u % 4
                return [[SQ5[:, u % 3, (2 * e + c) * P:(2 * e + c + 1) * P] for e in range(2)
                         for c in range(1 if blk == 0 else 0, 2)]]

            def sw_values(u):
                pair, blk = u // 4, u % 4
                at = 0
                for e in range(2):
                    for c in range(1 if blk == 0 else 0, 2):
                        last = nc.tensor.matmul(bank[64 * e:64 * e + 64, 6 + pair % 2, blk * P:(blk + 1) * P],
                                                VS[:, blk - 1 + c, 64 * (pair // 2):64 * (pair // 2) + 64],
                                                TMP5[:, u % 2, at * P:(at + 1) * P],
                                                start=(blk == 0 or c == 0), stop=(c == 1))
                        at += 1
                return last

            pe.wait_ge(gate["lf"], 1)
            attention(asw, 32, 2, sw_scores, sw_pieces, sw_values, 2, (4, 5), 2, 4)

            def og_chunk(b):
                at = 4 + b if b < 2 else 7
                n = BASE["o_m"] + b // 2
                if b % 2 == 0:
                    begin(n)
                if b >= 3:
                    pe.wait_ge(og["act"], b)
                for k in range(KC):
                    last = mm(bank[:, at, :], slot(n, ((b % 2) * KC + k) * P, P), H[:, k, 0:S], k == 0,
                              k == KC - 1, b % 2 == 0 and k == 0)
                last.then_inc(og["done"], 1)

            og_chunk(0)
            og_chunk(1)
            pe.wait_ge(asw["oc"], 8)
            pe.wait_ge(gate["rows"], 1)
            for c in range(4):
                last = nc.tensor.transpose(bank[:, 7, c * 4:(c + 1) * 4], ROWS[0:4, 2, c * P:(c + 1) * P],
                                           con("ident", 0, 4, 4))
            last.then_inc(gate["cols"], 1)
            pe.wait_ge(gate["ready"], 1)
            for h in range(X_HEADS):
                if h >= 1:
                    pe.wait_ge(ml["floor"], h)
                    pe.wait_ge(ml["root"], h)
                nc.tensor.matmul(bank[:, 0, :], con("select", h * P, P, 4), ROWS[0:4, 3, :], start=True, stop=True)
                nc.tensor.matmul(bank[:, 1, :], con("select", h * P, P, 4), ROWS[0:4, 4, :], start=True,
                                 stop=True).then_inc(ml["bcast"], 1)
                for c in range(5):
                    if c < 4:
                        if 4 * h + c >= 2:
                            pe.wait_ge(ml["w"], 4 * h + c - 1)
                        nc.tensor.matmul(bank[:, 2 + c % 2, 0:S - c * P], QK[:, 4 + h, c * P:(c + 1) * P],
                                         QK[:, h, c * P:S], start=True, stop=True).then_inc(ml["s"], 1)
                    if c >= 1:
                        d = c - 1
                        pe.wait_ge(ml["w"], 4 * h + d + 1)
                        if d == 0:
                            if h == 0:
                                pe.wait_ge(og["act"], 2)
                            else:
                                pe.wait_ge(ml["num"], h)
                        for v in range(2):
                            nc.tensor.matmul(bank[:, 4 + v, d * P:S], VX[:, d, (2 * h + v) * P:(2 * h + v + 1) * P],
                                             TMP5[:, d % 2, 0:S - d * P], start=(d == 0), stop=(d == 3))
                        nc.tensor.matmul(bank[:, 6, d * P:S], ones, TMP5[:, d % 2, 0:S - d * P], start=(d == 0),
                                         stop=(d == 3)).then_inc(ml["used"], 1)
                og_chunk(OG_IN[h][0])
                for v in range(2):
                    pe.wait_ge(ml["sq"], 2 * h + v + 1)
                    last = nc.tensor.matmul(bank[:, 0, :], ones, SQ5[:, v, :], start=(v == 0), stop=(v == 1))
                last.then_inc(ml["ssq"], 1)
                for b in OG_IN[h][1:]:
                    og_chunk(b)
            pe.wait_ge(ml["root"], X_HEADS)
            pe.wait_ge(og["act"], 8)
            merged(mrg2, "merge2", 8, YA, QS, og["free"])
            pe.wait_ge(mrg2["free"], 2 * KC)
            out_projection(out2, nmlp["xnew"], "out2", KC, MR2, LAT, 16, (nmlp, (6,)))

            def up3_round(i, first=False):
                for j in range(8):
                    n = BASE["up3"] + j // 2
                    if j % 2 == 0:
                        begin(n, i)
                    if not (first and j < 4):
                        pe.wait_ge(up3["free"], 8 * i + (j - 3))
                    for k in range(KC):
                        if first and j == 0:
                            pe.wait_ge(nmlp["ready"], nmlp["base"] + k + 1)
                        last = mm(bank[:, j % 4, :], slot(n, ((j % 2) * KC + k) * P, P), H[:, k, 0:S], k == 0,
                                  k == KC - 1, j % 2 == 0 and k == 0)
                    last.then_inc(up3["done"], 1)

            up3_round(0, True)
            rounds(pe, 1, FF2 // 8, up3_round)
            pe.wait_ge(up3["free"], FF2)
            out_projection(down3, nple["xnew"], "down3", FF2, HID2, LAT, 16, (nple, (6,)))

            pe.wait_ge(p_landed, 16)
            for o in range(KC):
                n = BASE["ple"] + o
                s = o % 2
                begin(n)
                if o >= 2:
                    pe.wait_ge(ple["free"], o - 1)
                for k in range(KC):
                    if o == 0:
                        pe.wait_ge(nple["ready"], nple["base"] + k + 1)
                    mm(bank[:, 2 * s, :], slot(n, k * P, P), H[:, k, 0:S], k == 0, k == KC - 1, k == 0)
                for k in range(2):
                    last = mm(bank[:, 2 * s + 1, :], slot(n, (KC + k) * P, P), PE2[:, k, :], k == 0, k == 1)
                last.then_inc(ple["done"], 1)
                if o >= 2:
                    sum_squares(nfin, o - 2, LAT, (6,)).then_inc(nfin["sq_used"], 1)
            for o in range(KC - 2, KC):
                sum_squares(nfin, o, LAT, (6,)).then_inc(nfin["sq_used"], 1)

        @block.scalar
        def _(act):
            A = nc.scalar.activation
            act.dma_start(CS, cB).then_inc(ada["c_landed"], 16)
            act.dma_start(prm[:, :], params).then_inc(inputs_landed, 16)
            act.dma_start(X[:, 0:4, :], xT[:, 0:4, :]).then_inc(inputs_landed, 16)
            act.dma_start(X[:, 4:8, :], xT[:, 4:8, :]).then_inc(inputs_landed, 16)
            act.dma_start(cst[:, :], consts).then_inc(inputs_landed, 16)

            def norm_squares(g, width, per_chunk):
                for k in range(KC):
                    if per_chunk:
                        act.wait_ge(g["xnew"], g["base"] + per_chunk * (k + 1))
                    if k >= 2:
                        act.wait_ge(g["sq_used"], g["base"] + k - 1)
                    A(SQ[:, k % 2, 0:width], X[:, k, 0:width], ACT.Square).then_inc(g["sq"], 1)

            def root(g, parts, banks, signal, features):
                for (a, b, _), n in zip(parts, banks):
                    A(rs[:, a:b], bank[:, n, 0:b - a], ACT.Sqrt, bias=eps, scale=1.0 / features).then_inc(signal, 1)

            def norm(g, parts, shift):
                act.wait_ge(g["sq_used"], g["base"] + KC)
                root(g, parts, (6, 5), g["root"], D)
                if shift is not None:
                    for k in range(KC):
                        for c, (a, b, col) in enumerate(parts):
                            act.wait_ge(g["scaled"], len(parts) * k + c + 1)
                            if shift == 0:
                                act.wait_ge(ada["got"], k + 2)
                            A(H[:, k, a:b], H[:, k, a:b], ACT.Identity,
                              bias=MODS[:, shift * KC + k, col:col + 1]).then_inc(g["ready"], 1)

            def post_norm(g, prev, parts):
                act.wait_ge(prev["sq_used"], prev["base"] + KC)
                root(g, parts, (4, 5), g["y_root"], D)
                norm_squares(g, parts[-1][1], len(parts))

            def swiglu(g, f, j, parts, peeled):
                act.wait_ge(g["done"], f + 1)
                if not peeled:
                    act.wait_ge(g["free"], f - 1)
                A(TMP[:, j, 0:S], bank[:, 3 * j, :], ACT.Silu).then_inc(g["act"], 1)
                if len(parts) == 2:
                    A(TMP[:, j, S:T], bank[:, 3 * j + 2, 0:CTX], ACT.Silu).then_inc(g["act"], 1)

            def down_out(g, o, j, parts, peeled):
                act.wait_ge(g["done"], o + (g["base"] + 1))
                if not peeled:
                    act.wait_ge(g["sq_used"], o + (g["base"] - 1))
                for a, b, c in parts:
                    last = A(SQ[:, j, a:b], bank[:, 2 * j + c, 0:b - a], ACT.Square)
                last.then_inc(g["sq"], 1)
                for a, b, c in parts:
                    dst = H[:, o, a:b] if isinstance(o, int) else \
                        H[:, bass.ds(o, 1), a:b].rearrange("p o t -> p (o t)")
                    last = A(dst, bank[:, 2 * j + c, 0:b - a], ACT.Copy)
                last.then_inc(g["free"], 1)

            def down(g, parts):
                def body(i, peeled=False):
                    for j in range(2):
                        down_out(g, 2 * i + j, j, parts, peeled)
                body(0, True)
                rounds(act, 1, KC // 2, body)

            def merge_gates(g, bias):
                for o in range(KC):
                    s = o % 2
                    act.wait_ge(g["done"], g["base"] + o + 1)
                    if o >= 2:
                        act.wait_ge(g["free"], g["base"] + o - 1)
                    for q, dst in ((0, SQ5), (1, TMP5)):
                        b = par("b_gate", q * KC + o) if bias else 0.0
                        A(dst[:, s, :], bank[:, 4 * s + q, :], ACT.Sigmoid, bias=b).then_inc(g["gate"], 1)

            def attention(g, units, exp_rows, pieces, turned_to, t_banks):
                upto = [0]
                for u in range(units):
                    upto.append(upto[-1] + len(pieces(u)))
                for i in range(units + 2):
                    if i < units:
                        act.wait_ge(g["max"], i + 1)
                        if i >= 3:
                            act.wait_ge(g["t"], upto[i - 2])
                        exp_rows(i)
                    if i >= 2:
                        u = i - 2
                        if u >= 2:
                            act.wait_ge(g["pv"], u - 1)
                        for q, width in enumerate(pieces(u)):
                            n = upto[u] + q
                            act.wait_ge(g["t"], n + 1)
                            A(turned_to(u, q, width), bank[:, t_banks[n % len(t_banks)], 0:width],
                              ACT.Copy).then_inc(g["tc"], 1)

            act.wait_ge(ada["c_landed"], 16)
            A(CS, CS, ACT.Silu).then_inc(ada["silu"], 1)
            act.wait_ge(inputs_landed, 16 * N_LOADS)
            norm_squares(n0, T, 0)
            norm(n0, BOTH, 0)

            def up1_act(i, peeled=False):
                for j in range(2):
                    swiglu(up1, 2 * i + j, j, BOTH, peeled)
            up1_act(0, True)
            rounds(act, 1, FF // 2, up1_act)
            act.wait_ge(up1["free"], FF)
            down(down1, BOTH)
            post_norm(na, down1, BOTH)
            norm(na, BOTH, 3)

            def proj_out(b):
                m = QK_D if b == 20 else P
                s = b % 3
                if b < 4:
                    return [q_blocks(b)]
                if 8 <= b < 12:
                    return v_blocks(b)
                if 12 <= b < 18:
                    return [(CQ[:, b - 12, :], bank[:, 2 * s, :])]
                dst = KR[0:m, :] if b == 20 else (KA if b < 8 else CKV)[:, b % 4 if b < 12 else b - 18, :]
                return [(dst[:, 0:S], bank[0:m, 2 * s, :]), (dst[:, S:T], bank[0:m, 2 * s + 1, 0:CTX])]

            for b in range(0, 21, 2):
                act.wait_ge(proj["done"], b + 1)
                pairs = proj_out(b)
                for dst, src in pairs:
                    last = A(dst, src, ACT.Copy, scale=NA_D ** -0.5 if b < 4 else 1.0)
                last.then_inc(proj["act"], 1)
            for v in range(0, 10, 2):
                act.wait_ge(vt["done"], v + 1)
                A(VN[:, v, :], bank[:, v % 4, :], ACT.Copy).then_inc(vt["act"], 1)

            def stat_col(u, i, n=1):
                return stat[:, 16 * (u % 4) + i:16 * (u % 4) + i + n]

            def na_exp(u):
                A(SQ5[:, u % 3, :], bank[:, NA_S[u % 3], :], ACT.Exp, bias=stat_col(u, 0),
                  accum_out=stat_col(u, 2)).then_inc(ana["exp"], 1)

            attention(ana, NA_HEADS * N_BLK, na_exp, lambda u: [512], lambda u, q, w: TMP[:, u % 2, 0:w], (2, 3))

            act.wait_ge(proj["dve"], 10)
            act.wait_ge(ana["t"], NA_HEADS * N_BLK)
            for k in range(QR + KVR):
                if k >= 2:
                    act.wait_ge(lora["sq_used"], k - 1)
                src, w = (CQ[:, k, :], S) if k < QR else (CKV[:, k - QR, :], T)
                A(SQ[:, k % 2, 0:w], src, ACT.Square).then_inc(lora["sq"], 1)
                if k == QR:
                    act.wait_ge(lora["sq_used"], QR)
                    act.wait_ge(ana["pv"], NA_HEADS * N_BLK)
                    A(TMP[:, 0, 0:S], bank[:, 0, :], ACT.Sqrt, bias=eps,
                      scale=1.0 / ML_Q_RANK).then_inc(lora["root"], 1)
            act.wait_ge(lora["sq_used"], QR + KVR)
            A(rs[:, 0:S], bank[:, 1, :], ACT.Sqrt, bias=eps, scale=1.0 / ML_KV_RANK).then_inc(lora["root"], 1)
            A(rs[:, S:T], bank[:, 2, 0:CTX], ACT.Sqrt, bias=eps, scale=1.0 / ML_KV_RANK).then_inc(lora["root"], 1)
            act.wait_ge(ana["oc"], NA_HEADS)
            for h in range(NA_HEADS):
                act.wait_ge(gen["q"], h + 1)
                A(QM[0:QK_D, h, :], bank[0:QK_D, 4 + h % 2, :], ACT.Copy, scale=QK_D ** -0.5).then_inc(gen["qc"], 1)
            for h in range(NA_HEADS):
                act.wait_ge(gen["k"], h + 1)
                A(KM[0:NOPE, h, 0:S], bank[0:NOPE, 2 * (h % 2), :], ACT.Copy)
                A(KM[0:NOPE, h, S:T], bank[0:NOPE, 2 * (h % 2) + 1, 0:CTX], ACT.Copy).then_inc(gen["kc"], 1)

            def mla_exp(u):
                s = u % 2
                A(PM[:, u % 3, :], bank[:, 2 * s:2 * s + 2, :].rearrange("p a b -> p (a b)")[:, 0:T], ACT.Exp,
                  bias=stat_col(u, 0), accum_out=stat_col(u, 2)).then_inc(amla["exp"], 1)

            attention(amla, NA_HEADS * 4, mla_exp, lambda u: [384, 384],
                      lambda u, q, w: TMP[:, u % 2, q * w:(q + 1) * w], (4, 5))
            act.wait_ge(amla["pv"], NA_HEADS * 4)
            merge_gates(mrg1, True)
            act.wait_ge(mrg1["free"], KC)
            down(out1, LAT)
            post_norm(nb, out1, LAT)
            norm(nb, LAT, 6)

            def up2_act(i, peeled=False):
                for j in range(2):
                    swiglu(up2, 2 * i + j, j, LAT, peeled)
            up2_act(0, True)
            rounds(act, 1, FF // 2, up2_act)
            act.wait_ge(up2["free"], FF)
            down(down2, LAT)
            post_norm(nmix, down2, LAT)
            norm(nmix, LAT, None)

            for b in range(8):
                act.wait_ge(conv["mixed"], b + 1)
                A(QK[:, b, :], TMP5[:, b % 2, :], ACT.Silu).then_inc(conv["ready"], 1)
            for b in range(0, 20, 2):
                act.wait_ge(prj2["done"], b + 1)
                if b < 8:
                    A(VX[:, 0:2, (b // 2) * 256:(b // 2 + 1) * 256],
                      bank[:, b % 4, :].rearrange("p (t n) -> p t n", t=2), ACT.Copy).then_inc(prj2["act"], 1)
                elif b < 16:
                    A(QS[:, b - 8, :], bank[:, b % 4, :], ACT.Copy, scale=SW_D ** -0.5).then_inc(prj2["act"], 1)
                elif b == 16:
                    for q in range(4):
                        last = A(KS[64 * (q // 2):64 * (q // 2) + 64, q % 2, :],
                                 bank[64 * (q % 2):64 * (q % 2) + 64, b % 4, :], ACT.Copy)
                    last.then_inc(prj2["act"], 1)
                else:
                    A(VS[:, 0:2, :], bank[:, b % 4, :].rearrange("p (t n) -> p t n", t=2),
                      ACT.Copy).then_inc(prj2["act"], 1)

            def sw_exp(u):
                s, lo = u % 3, (P if u % 4 == 0 else 0)
                for e in range(2):
                    A(SQ5[:, s, e * 256 + lo:(e + 1) * 256], bank[:, 2 * (u % 2) + e, lo:256], ACT.Exp,
                      bias=stat_col(u, e), accum_out=stat_col(u, 2 + e)).then_inc(asw["exp"], 1)
                A(stat_col(u, 6, 2), stat_col(u, 4, 2), ACT.Exp).then_inc(asw["biased"], 1)

            attention(asw, 32, sw_exp, lambda u: [256 if u % 4 == 0 else 512],
                      lambda u, q, w: TMP5[:, u % 2, 0:w], (4, 5))

            act.wait_ge(gate["lf"], 2)
            A(ROWS[0:4, 5, :], ROWS[0:4, 5, :], ACT.Exp, scale=-1.0).then_inc(gate["exp"], 1)
            act.wait_ge(gate["exp"], 1)
            A(ROWS[0:4, 5, :], ROWS[0:4, 5, :], ACT.Ln, bias=con("ones", 0, 1, 4)).then_inc(gate["soft"], 1)

            def og_rows(b):
                act.wait_ge(og["done"], b + 1)
                A(OG[b], bank[:, 4 + b if b < 2 else 7, :], ACT.Copy).then_inc(og["act"], 1)
            og_rows(0)
            og_rows(1)
            for h in range(X_HEADS):
                act.wait_ge(ml["bcast"], h + 1)
                if h == 0:
                    act.wait_ge(gate["ready"], 1)
                A(rs[:, 0:S], bank[:, 0, :], ACT.Copy, scale=-1.0).then_inc(ml["minus_m"], 1)
                for c in range(4):
                    n = 4 * h + c
                    act.wait_ge(ml["minus_m"], h + 1)
                    act.wait_ge(ml["diag"], n + 1)
                    if c < 3:
                        A(SQ5[:, c % 2, P:S - c * P], rs[:, (c + 1) * P:S], ACT.Exp, bias=ACOL[:, c, h:h + 1])
                    A(SQ5[:, c % 2, 0:P], SQ5[:, c % 2, 0:P], ACT.Exp, bias=ACOL[:, c, h:h + 1]).then_inc(ml["e"], 1)
                if h >= 1:
                    for b in OG_IN[h - 1][1:]:
                        og_rows(b)
                act.wait_ge(ml["w"], 4 * h + 4)
                A(SQ5[:, 2, :], bank[:, 1, :], ACT.Exp, scale=-1.0).then_inc(ml["floor"], 1)
                act.wait_ge(ml["used"], 4 * h + 4)
                A(TMP5[:, 2, :], bank[:, 6, :], ACT.Abs).then_inc(ml["acc"], 1)
                for v in range(2):
                    act.wait_ge(ml["num"], h + 1)
                    A(SQ5[:, v, :], YA[:, 2 * h + v, :], ACT.Square).then_inc(ml["sq"], 1)
                act.wait_ge(ml["ssq"], h + 1)
                A(rs[:, 0:S], bank[:, 0, :], ACT.Sqrt, bias=eps, scale=1.0 / X_DV).then_inc(ml["root"], 1)
                og_rows(OG_IN[h][0])
                if h < X_HEADS - 1:
                    act.wait_ge(ml["head"], h + 1)
            for b in range(8):
                if b == 7:
                    og_rows(b)
                act.wait_ge(og["act"], b + 1)
                A(OG[b], OG[b], ACT.Sigmoid).then_inc(og["gate"], 1)
            act.wait_ge(ml["head"], X_HEADS)
            merge_gates(mrg2, False)
            act.wait_ge(mrg2["free"], 2 * KC)
            norm_squares(nmlp, S, 1)
            norm(nmlp, LAT, None)

            def up3_act(i, peeled=False):
                for j in range(8):
                    act.wait_ge(up3["done"], 8 * i + j + 1)
                    dst = HID2[:, 8 * i + j, :] if isinstance(i, int) else \
                        HID2[:, bass.ds(8 * i + j, 1), :].rearrange("p o t -> p (o t)")
                    A(dst, bank[:, j % 4, :], ACT.Relu).then_inc(up3["act"], 1)
            rounds(act, 0, FF2 // 8, up3_act)
            norm_squares(nple, S, 1)
            norm(nple, LAT, None)

            for o in range(KC + 1):
                if o < KC:
                    act.wait_ge(ple["done"], o + 1)
                    if o >= 2:
                        act.wait_ge(nfin["xnew"], nfin["base"] + o - 1)
                    A(TMP5[:, o % 2, :], bank[:, 2 * (o % 2), :], ACT.Sigmoid).then_inc(ple["gate"], 1)
                if o >= 1:
                    k = o - 1
                    act.wait_ge(nfin["xnew"], nfin["base"] + k + 1)
                    if k >= 2:
                        act.wait_ge(nfin["sq_used"], nfin["base"] + k - 1)
                    A(SQ[:, k % 2, 0:S], X[:, k, 0:S], ACT.Square).then_inc(nfin["sq"], 1)
            norm(nfin, LAT, None)

        @block.vector
        def _(dve):
            V = nc.vector
            chain = [0]

            def link(ins):
                chain[0] += 1
                ins.then_inc(dve_c, 1)
                dve.wait_ge(dve_c, chain[0])

            def mark(ins):
                chain[0] += 1
                ins.then_inc(dve_c, 1)
                return chain[0]

            def norm(g, parts, scale, shifted):
                dve.wait_ge(g["root"], g["turn"] + len(parts))
                width = parts[-1][1]
                link(V.reciprocal(rs[:, 0:width], rs[:, 0:width]))
                for k in range(KC):
                    for a, b, col in parts:
                        V.scalar_tensor_tensor(H[:, k, a:b], X[:, k, a:b], scale(k, col), rs[:, a:b], ALU.mult,
                                               ALU.mult).then_inc(g["scaled"] if shifted else g["ready"], 1)

            def post_norm(g, parts, gate_row):
                dve.wait_ge(g["y_root"], len(parts))
                width = parts[-1][1]
                link(V.reciprocal(rs[:, 0:width], rs[:, 0:width]))
                marks = {}
                for k in range(KC + 1):
                    if k < KC:
                        if k >= 2:
                            dve.wait_ge(g["xnew"], len(parts) * (k - 1))
                        for a, b, col in parts:
                            marks[k, col] = mark(V.scalar_tensor_tensor(
                                TMP[:, k % 2, a:b], H[:, k, a:b], COEF[:, gate_row, k, col:col + 1], rs[:, a:b],
                                ALU.mult, ALU.mult))
                    if k >= 1:
                        for a, b, col in parts:
                            dve.wait_ge(dve_c, marks[k - 1, col])
                            V.tensor_tensor(X[:, k - 1, a:b], X[:, k - 1, a:b], TMP[:, (k - 1) % 2, a:b],
                                            ALU.add).then_inc(g["xnew"], 1)

            def modulated(row):
                return lambda k, col: COEF[:, row, k, col:col + 1]

            def plain(name):
                return lambda k, col: par(name, k)

            def mods_of(i):
                return MODS[:, i * KC:(i + 1) * KC, :]

            def norm_g(i):
                return par("norm_g", i * 2 * KC, 2 * KC).rearrange("p (k c) -> p k c", c=2)

            def scale_coef(row, m, g):
                return V.scalar_tensor_tensor(COEF[:, row, :, :], mods_of(m), 1.0, norm_g(g), ALU.add, ALU.mult)

            def gate_coef(row, m, weight, g):
                return V.scalar_tensor_tensor(COEF[:, row, :, :], mods_of(m), weight, norm_g(g), ALU.mult, ALU.mult)

            def ada_products(m, w, acc):
                for c in range(2):
                    if not (isinstance(m, int) and m + c == 0):
                        dve.wait_ge(ada["done"], m * 2 + c)
                    V.tensor_tensor_reduce(p_sb[:, :], w, CS[:, c, :], 1.0, 0.0, ALU.mult, ALU.add,
                                           acc[:, c:c + 1]).then_inc(ada["done"], 1)

            def ada_add(m, n, acc):
                if isinstance(m, int):
                    dst, bias = mods_t[:, m:m + n], par("b_ada", m, n)
                else:
                    dst, bias = mods_t[:, bass.ds(m, n)], prm[:, bass.ds(m + PARAM["b_ada"], n)]
                V.tensor_tensor(dst, acc, bias, ALU.add).then_inc(ada["got"], 1)

            def ada_pair(t, s, turn):
                dve.wait_ge(ada["pair_landed%d" % s], turn * 32 + 32)
                dve.wait_ge(ada["got"], t + KC)
                for q in range(2):
                    ada_products(t * 2 + (2 * KC + q), ADA_PAIR[s][q], ada_acc[:, 4 * s + 2 * q:4 * s + 2 * q + 2])
                dve.wait_ge(ada["done"], t * 4 + (4 * KC + 4))
                ada_add(t * 4 + 4 * KC, 4, ada_acc[:, 4 * s:4 * s + 4])

            def product(g, f, j, parts):
                def hid(a, b):
                    return HID[:, f, a:b] if isinstance(f, int) else \
                        HID[:, bass.ds(f, 1), a:b].rearrange("p o t -> p (o t)")
                n = len(parts)
                dve.wait_ge(g["act"], n * f + 1)
                if n == 2:
                    V.tensor_tensor(hid(0, S), TMP[:, j, 0:S], bank[:, 3 * j + 1, :], ALU.mult)
                    dve.wait_ge(g["act"], n * f + 2)
                    V.tensor_tensor(hid(S, T), TMP[:, j, S:T], bank[:, 3 * j + 2, CTX:2 * CTX],
                                    ALU.mult).then_inc(g["free"], 1)
                else:
                    V.tensor_tensor(hid(0, S), TMP[:, j, 0:S], bank[:, 3 * j + 1, :], ALU.mult).then_inc(g["free"], 1)

            def residual_add(g, done, o, j):
                dve.wait_ge(done, o + (g["base"] + 1))
                x = X[:, o, 0:S] if isinstance(o, int) else X[:, bass.ds(o, 1), 0:S].rearrange("p o t -> p (o t)")
                V.tensor_tensor(x, x, bank[:, 2 * j, :], ALU.add).then_inc(g["xnew"], 1)

            def residual_adds(g, done):
                def body(i):
                    for j in range(2):
                        residual_add(g, done, 2 * i + j, j)
                rounds(dve, 0, KC // 2, body)

            def merge(g, dst):
                for o in range(KC):
                    s = o % 2
                    dve.wait_ge(g["gate"], 2 * (g["base"] + o) + 1)
                    mark(V.tensor_tensor(SQ5[:, s, :], SQ5[:, s, :], bank[:, 4 * s + 2, :], ALU.mult))
                    dve.wait_ge(g["gate"], 2 * (g["base"] + o) + 2)
                    link(V.tensor_tensor(TMP5[:, s, :], TMP5[:, s, :], bank[:, 4 * s + 3, :], ALU.mult))
                    V.tensor_tensor(dst[:, o, :], SQ5[:, s, :], TMP5[:, s, :], ALU.add).then_inc(g["free"], 1)

            def stat_col(u, i, n=1):
                return stat[:, 16 * (u % 4) + i:16 * (u % 4) + i + n]

            def attention(g, units, maxima, normalise, per_out, take):
                for i in range(units + 4):
                    u = i - 4
                    if u >= 0 and u % per_out == per_out - 1:
                        dve.wait_ge(g["pv"], u + 1)
                        take(u // per_out).then_inc(g["oc"], 1)
                    if i < units:
                        dve.wait_ge(g["s"], i + 1)
                        maxima(i)
                    if 1 <= i <= units:
                        normalise(i - 1)

            dve.wait_ge(ada["silu"], 1)
            for k in range(KC):
                if k % 4 == 0:
                    dve.wait_ge(ada["landed%d" % (k // 4)], 16)
                ada_products(k, ADA_HEAD[:, KC + k, :], mods_t[:, 2 * (KC + k):2 * (KC + k) + 2])
            dve.wait_ge(ada["done"], 2 * KC)
            dve.wait_ge(inputs_landed, 16 * N_LOADS)
            ada_add(2 * KC, 2 * KC, mods_t[:, 2 * KC:4 * KC])
            dve.wait_ge(ada["got"], 1)
            link(scale_coef(SCALE1, 1, 0))
            dve.wait_ge(n0["root"], 2)
            link(V.reciprocal(rs[:, :], rs[:, :]))
            for k in range(KC):
                if k % 4 == 0:
                    dve.wait_ge(ada["landed%d" % (2 + k // 4)], 16)
                ada_products(KC + k, ADA_HEAD[:, k, :], mods_t[:, 2 * k:2 * k + 2])
                dve.wait_ge(ada["done"], 2 * (KC + k) + 2)
                ada_add(2 * k, 2, mods_t[:, 2 * k:2 * k + 2])
                for a, b, col in BOTH:
                    V.scalar_tensor_tensor(H[:, k, a:b], X[:, k, a:b], COEF[:, SCALE1, k, col:col + 1], rs[:, a:b],
                                           ALU.mult, ALU.mult).then_inc(n0["scaled"], 1)

            def up1_dve(i):
                for j in range(2):
                    product(up1, 2 * i + j, j, BOTH)
                    ada_pair(2 * i + j, j, i)
            rounds(dve, 0, FF // 2, up1_dve)
            for t in range(FF, 28):
                ada_pair(t, t % 2, t // 2)
            dve.wait_ge(ada["got"], 1 + KC + 28)
            mark(gate_coef(GATE1, 2, 0.5, 1))
            mark(scale_coef(SCALE2, 4, 2))
            mark(gate_coef(GATE2, 5, 1.0, 3))
            mark(scale_coef(SCALE3, 7, 4))
            link(gate_coef(GATE3, 8, 0.5, 5))
            dve.wait_ge(down1["free"], KC)
            post_norm(na, BOTH, GATE1)
            norm(na, BOTH, modulated(SCALE2), True)

            for b in range(1, 21, 2):
                dve.wait_ge(proj["done"], b + 1)
                s = b % 3
                if b < 4:
                    dst, src = q_blocks(b)
                    V.tensor_scalar(dst, src, NA_D ** -0.5, None, ALU.mult).then_inc(proj["dve"], 1)
                elif 8 <= b < 12:
                    for dst, src in v_blocks(b):
                        ins = V.tensor_copy(dst, src)
                    ins.then_inc(proj["dve"], 1)
                elif 12 <= b < 18:
                    V.tensor_copy(CQ[:, b - 12, :], bank[:, 2 * s, :]).then_inc(proj["dve"], 1)
                else:
                    dst = (KA if b < 8 else CKV)[:, b % 4 if b < 12 else b - 18, :]
                    mark(V.tensor_copy(dst[:, 0:S], bank[:, 2 * s, :]))
                    V.tensor_copy(dst[:, S:T], bank[:, 2 * s + 1, 0:CTX]).then_inc(proj["dve"], 1)
            for v in range(1, 10, 2):
                dve.wait_ge(vt["done"], v + 1)
                V.tensor_copy(VN[:, v, :], bank[:, v % 4, :]).then_inc(vt["dve"], 1)

            def na_maxima(u):
                dve.wait_ge(ana["bias"], u + 1)
                ins = V.tensor_tensor(bank[:, NA_S[u % 3], 0:256], bank[:, NA_S[u % 3], 0:256],
                                      bm_t[:, 256 * (u % 2):256 * (u % 2) + 256], ALU.add)
                ins.then_inc(ana["biased"], 1)
                dve.wait_ge(ana["biased"], u + 1)
                V.tensor_reduce(stat_col(u, 0), bank[:, NA_S[u % 3], :], AX.X, ALU.max, negate=True).then_inc(ana["max"], 1)

            def plain_normalise(g, rows, width):
                def run(u):
                    dve.wait_ge(g["exp"], u + 1)
                    link(V.reciprocal(stat_col(u, 3), stat_col(u, 2)))
                    V.tensor_scalar(rows[:, u % 3, 0:width], rows[:, u % 3, 0:width], stat_col(u, 3), None,
                                    ALU.mult).then_inc(g["norm"], 1)
                return run

            def na_take(h):
                e = NA_D * (h % 2)
                dst = QA[e:e + NA_D, h // 2, :].rearrange("p (r j c) -> p j r c", r=GRID_H, j=N_BLK)
                src = bank[e:e + NA_D, 4 + h % 2, :].rearrange("p (j r c) -> p j r c", j=N_BLK, r=GRID_H)
                return V.tensor_copy(dst, src)

            attention(ana, NA_HEADS * N_BLK, na_maxima, plain_normalise(ana, SQ5, 512), N_BLK, na_take)

            dve.wait_ge(lora["root"], 1)
            link(V.reciprocal(TMP[:, 0, 0:S], TMP[:, 0, 0:S]))
            for k in range(QR):
                V.scalar_tensor_tensor(CQ[:, k, :], CQ[:, k, :], par("g_q", k), TMP[:, 0, 0:S], ALU.mult,
                                       ALU.mult).then_inc(lora["normed"], 1)
            dve.wait_ge(lora["root"], 3)
            link(V.reciprocal(rs[:, :], rs[:, :]))
            for k in range(KVR):
                V.scalar_tensor_tensor(CKV[:, k, :], CKV[:, k, :], par("g_kv", k), rs[:, :], ALU.mult,
                                       ALU.mult).then_inc(lora["normed"], 1)
            dve.wait_ge(lora["normed"], QR + KVR)
            dve.wait_ge(gen["kr"], 1)
            mark(V.tensor_tensor(TMP[0:QK_D, 1, 0:S], bank[0:QK_D, 3, :], con("sin", 0, S, QK_D), ALU.mult))
            link(V.tensor_tensor(KR[0:QK_D, 0:S], KR[0:QK_D, 0:S], con("cos", 0, S, QK_D), ALU.mult))
            link(V.tensor_tensor(KR[0:QK_D, 0:S], KR[0:QK_D, 0:S], TMP[0:QK_D, 1, 0:S], ALU.add))
            for h in range(NA_HEADS):
                last = V.tensor_copy(KM[NOPE:QK_D, h, :], KR[NOPE:QK_D, :])
                if h < NA_HEADS - 1:
                    mark(last)
            last.then_inc(gen["kr_roped"], 1)
            for h in range(NA_HEADS):
                dve.wait_ge(gen["rot"], h + 1)
                mark(V.tensor_tensor(TMP5[0:QK_D, h % 2, :], bank[0:QK_D, 6 + h % 2, :], con("sin", 0, S, QK_D),
                                     ALU.mult))
                link(V.tensor_tensor(QM[0:QK_D, h, :], QM[0:QK_D, h, :], con("cos", 0, S, QK_D), ALU.mult))
                V.tensor_tensor(QM[0:QK_D, h, :], QM[0:QK_D, h, :], TMP5[0:QK_D, h % 2, :],
                                ALU.add).then_inc(gen["q_roped"], 1)
            for t in range(6):
                dve.wait_ge(gen["v"], t + 1)
                V.tensor_copy(VM[:, t, :], bank[:, 4 + t % 2, :]).then_inc(gen["vc"], 1)

            def mla_maxima(u):
                s = u % 2
                V.tensor_reduce(stat_col(u, 0), bank[:, 2 * s:2 * s + 2, :].rearrange("p a b -> p (a b)")[:, 0:T],
                                AX.X, ALU.max, negate=True).then_inc(amla["max"], 1)

            def mla_take(h):
                e = V_D * (h % 2)
                return V.tensor_copy(OM[e:e + V_D, h // 2, :], bank[e:e + V_D, 6 + h % 2, :])

            attention(amla, NA_HEADS * 4, mla_maxima, plain_normalise(amla, PM, T), 4, mla_take)
            merge(mrg1, MR1)
            dve.wait_ge(out1["free"], 2 * KC)
            post_norm(nb, LAT, GATE2)
            norm(nb, LAT, modulated(SCALE3), True)

            def up2_dve(i):
                for j in range(2):
                    product(up2, 2 * i + j, j, LAT)
            rounds(dve, 0, FF // 2, up2_dve)
            dve.wait_ge(down2["free"], 3 * KC)
            post_norm(nmix, LAT, GATE3)
            norm(nmix, LAT, plain("mix_g"), False)

            for b in range(8):
                dve.wait_ge(conv["raw"], b + 1)
                if b >= 2:
                    dve.wait_ge(conv["ready"], b - 1)
                acc = TMP5[:, b % 2, :]
                link(V.tensor_scalar(acc, bank[:, b % 4, :], par("conv", 4 * b + 3), None, ALU.mult))
                for back in range(1, 4):
                    ins = V.scalar_tensor_tensor(acc[:, back:S], bank[:, b % 4, 0:S - back],
                                                 par("conv", 4 * b + 3 - back), acc[:, back:S], ALU.mult, ALU.add)
                    if back < 3:
                        link(ins)
                ins.then_inc(conv["mixed"], 1)
            for b in range(1, 20, 2):
                dve.wait_ge(prj2["done"], b + 1)
                if b < 8:
                    V.tensor_copy(VX[:, 2:4, (b // 2) * 256:(b // 2 + 1) * 256],
                                  bank[:, b % 4, :].rearrange("p (t n) -> p t n", t=2)).then_inc(prj2["dve"], 1)
                elif b < 16:
                    V.tensor_scalar(QS[:, b - 8, :], bank[:, b % 4, :], SW_D ** -0.5, None,
                                    ALU.mult).then_inc(prj2["dve"], 1)
                elif b == 17:
                    for q in range(4):
                        ins = V.tensor_copy(KS[64 * (q // 2):64 * (q // 2) + 64, 2 + q % 2, :],
                                            bank[64 * (q % 2):64 * (q % 2) + 64, b % 4, :])
                        if q < 3:
                            mark(ins)
                    ins.then_inc(prj2["dve"], 1)
                else:
                    V.tensor_copy(VS[:, 2:4, :], bank[:, b % 4, :].rearrange("p (t n) -> p t n", t=2)
                                  ).then_inc(prj2["dve"], 1)
            dve.wait_ge(gate["pre"], 1)
            mark(V.tensor_scalar(YA[0:4, 0, :], bank[0:4, 6, :], par("b_if", 0, 1, 4), None, ALU.add))
            V.tensor_scalar(YA[0:4, 1, :], bank[32:36, 6, :], prm[32:36, PARAM["b_if"] + 1:PARAM["b_if"] + 2],
                            None, ALU.add).then_inc(gate["lf"], 1)

            def sw_maxima(u):
                s, pair, lo = u % 2, u // 4, (P if u % 4 == 0 else 0)
                rows = bank[:, 2 * s:2 * s + 2, lo:256]
                mask = con("sw_mask", lo, 256 - lo).unsqueeze(1).to_broadcast([P, 2, 256 - lo])
                link(V.tensor_tensor(rows, rows, mask, ALU.add))
                link(V.tensor_reduce(stat_col(u, 8, 2), rows, AX.X, ALU.max))
                link(V.tensor_tensor(stat_col(u, 8, 2), stat_col(u, 8, 2), par("sinks", 2 * pair, 2), ALU.max))
                mark(V.tensor_scalar(stat_col(u, 0, 2), stat_col(u, 8, 2), -1.0, None, ALU.mult))
                V.tensor_tensor(stat_col(u, 4, 2), par("sinks", 2 * pair, 2), stat_col(u, 8, 2),
                                ALU.subtract).then_inc(asw["max"], 1)

            def sw_normalise(u):
                dve.wait_ge(asw["biased"], u + 1)
                link(V.tensor_tensor(stat_col(u, 10, 2), stat_col(u, 2, 2), stat_col(u, 6, 2), ALU.add))
                link(V.reciprocal(stat_col(u, 10, 2), stat_col(u, 10, 2)))
                lo = P if u % 4 == 0 else 0
                for e in range(2):
                    p = SQ5[:, u % 3, e * 256 + lo:(e + 1) * 256]
                    ins = V.tensor_scalar(p, p, stat_col(u, 10 + e), None, ALU.mult)
                    if e == 0:
                        mark(ins)
                ins.then_inc(asw["norm"], 1)

            attention(asw, 32, sw_maxima, sw_normalise, 4, lambda p: V.tensor_copy(QS[:, p, :], bank[:, 6 + p % 2, :]))

            link(V.tensor_copy(ROWS[0:4, 0:2, :], YA[0:4, 0:2, :]))
            link(V.tensor_scalar(ROWS[0:4, 5, :], ROWS[0:4, 1, :], -1.0, None, ALU.mult))
            V.tensor_tensor(ROWS[0:4, 5, :], ROWS[0:4, 5, :], ROWS[0:4, 1, :], ALU.max).then_inc(gate["lf"], 1)
            link(V.memset(YA[0:4, 2, :], 1.0))
            dve.wait_ge(gate["soft"], 1)
            link(V.scalar_tensor_tensor(ROWS[0:4, 1, :], ROWS[0:4, 1, :], 0.0, ROWS[0:4, 5, :], ALU.min, ALU.subtract))
            link(V.tensor_tensor_scan(ROWS[0:4, 5, :], YA[0:4, 2, :], ROWS[0:4, 1, :], 0.0, ALU.mult, ALU.add))
            link(V.tensor_tensor(ROWS[0:4, 2, :], ROWS[0:4, 0, :], ROWS[0:4, 5, :], ALU.subtract))
            link(V.tensor_tensor_scan(ROWS[0:4, 3, :], ROWS[0:4, 2, :], ROWS[0:4, 2, :], 0.0, ALU.max, ALU.max))
            V.tensor_tensor(ROWS[0:4, 4, :], ROWS[0:4, 3, :], ROWS[0:4, 5, :], ALU.add).then_inc(gate["rows"], 1)
            dve.wait_ge(gate["cols"], 1)
            V.tensor_copy(ACOL, bank[:, 7, 0:16].rearrange("p (c h) -> p c h", c=4)).then_inc(gate["ready"], 1)
            for h in range(X_HEADS):
                dve.wait_ge(ml["minus_m"], h + 1)
                for c in range(5):
                    if c < 4:
                        if c < 2 and h >= 1:
                            dve.wait_ge(ml["ssq"], h)
                        if c >= 2:
                            dve.wait_ge(ml["w"], 4 * h + c - 1)
                        V.tensor_tensor(SQ5[:, c % 2, 0:P], rs[:, c * P:(c + 1) * P], con("causal", 0, P),
                                        ALU.add).then_inc(ml["diag"], 1)
                    if c >= 1:
                        d = c - 1
                        dve.wait_ge(ml["e"], 4 * h + d + 1)
                        dve.wait_ge(ml["s"], 4 * h + d + 1)
                        if 4 * h + d >= 2:
                            dve.wait_ge(ml["used"], 4 * h + d - 1)
                        V.scalar_tensor_tensor(TMP5[:, d % 2, 0:S - d * P], bank[:, 2 + d % 2, 0:S - d * P],
                                               X_DK ** -0.5, SQ5[:, d % 2, 0:S - d * P], ALU.mult,
                                               ALU.mult).then_inc(ml["w"], 1)
                dve.wait_ge(ml["floor"], h + 1)
                dve.wait_ge(ml["acc"], h + 1)
                link(V.tensor_tensor(SQ5[:, 2, :], SQ5[:, 2, :], TMP5[:, 2, :], ALU.max))
                link(V.reciprocal(SQ5[:, 2, :], SQ5[:, 2, :]))
                mark(V.tensor_tensor(YA[:, 2 * h, :], bank[:, 4, :], SQ5[:, 2, :], ALU.mult))
                V.tensor_tensor(YA[:, 2 * h + 1, :], bank[:, 5, :], SQ5[:, 2, :], ALU.mult).then_inc(ml["num"], 1)
                dve.wait_ge(ml["root"], h + 1)
                link(V.reciprocal(rs[:, 0:S], rs[:, 0:S]))
                for v in range(2):
                    ins = V.scalar_tensor_tensor(YA[:, 2 * h + v, :], YA[:, 2 * h + v, :], par("mlstm_g", 2 * h + v),
                                                 rs[:, 0:S], ALU.mult, ALU.mult)
                    if v == 0:
                        mark(ins)
                ins.then_inc(ml["head"], 1)
            for b in range(8):
                dve.wait_ge(og["gate"], b + 1)
                if b == 0:
                    dve.wait_ge(ml["head"], X_HEADS)
                V.tensor_tensor(YA[:, b, :], YA[:, b, :], OG[b], ALU.mult).then_inc(og["free"], 1)
            merge(mrg2, MR2)
            residual_adds(nmlp, out2["done"])
            norm(nmlp, LAT, plain("mlp_g"), False)

            def up3_dve(i):
                for j in range(8):
                    dve.wait_ge(up3["act"], 8 * i + j + 1)
                    h = HID2[:, bass.ds(8 * i + j, 1), :].rearrange("p o t -> p (o t)")
                    V.scalar_tensor_tensor(h, bank[:, j % 4, :], 0.0, h, ALU.max, ALU.mult).then_inc(up3["free"], 1)
            rounds(dve, 0, FF2 // 8, up3_dve)
            residual_adds(nple, down3["done"])
            norm(nple, LAT, plain("ple_g"), False)
            for o in range(KC):
                s = o % 2
                dve.wait_ge(ple["gate"], o + 1)
                V.tensor_tensor(TMP5[:, s, :], TMP5[:, s, :], bank[:, 2 * s + 1, :], ALU.mult).then_inc(ple["free"], 1)
                dve.wait_ge(ple["free"], o + 1)
                V.tensor_tensor(X[:, o, 0:S], X[:, o, 0:S], TMP5[:, s, :], ALU.add).then_inc(nfin["xnew"], 1)
            norm(nfin, LAT, plain("final_g"), False)

        @block.gpsimd
        def _(pool):
            for k in range(0, 2 * KC, 4):
                at = (k + KC) % (2 * KC)
                pool.dma_start(ADA_HEAD[:, at:at + 4, :], w_ada[:, at:at + 4, :]).then_inc(ada["landed%d" % (k // 4)], 16)

            def pairs(i, first=False):
                for s in range(2):
                    if not first:
                        pool.wait_ge(ada["done"], i * 8 + (4 * KC + 4 * s - 4))
                    for q in range(2):
                        m = 4 * i + 2 * KC + 2 * s + q if first else bass.ds(i * 4 + (2 * KC + 2 * s + q), 1)
                        src = w_ada[:, m, :] if first else w_ada[:, m, :].rearrange("p o d -> p (o d)")
                        pool.dma_start(ADA_PAIR[s][q], src).then_inc(ada["pair_landed%d" % s], 16)
            pairs(0, True)
            rounds(pool, 1, 14, pairs)
            pool.wait_ge(ada["done"], 2 * N_MOD * KC)
            pool.dma_start(bias_t[:, :], rpb).then_inc(rpb_landed, 16)
            pool.wait_ge(inputs_landed, 16 * N_LOADS)
            pool.wait_ge(rpb_landed, 16)
            for u in range(NA_HEADS * N_BLK):
                h, j = u // N_BLK, u % N_BLK
                if u >= 2:
                    pool.wait_ge(ana["biased"], u - 1)
                at = K_START[j] - Q_COLS * j + Q_COLS
                nc.gpsimd.tensor_tensor(bm_t[:, 256 * (u % 2):256 * (u % 2) + 256].rearrange("p (a k) -> p a k", a=8),
                                        BIAS[:, h, :, at:at + K_COLS], con("na_mask", j * K_COLS, K_COLS).unsqueeze(1)
                                        .to_broadcast([P, GRID_H, K_COLS]), ALU.add).then_inc(ana["bias"], 1)
            pool.wait_ge(og["free"], 8)
            pool.dma_start(PE2, pT).then_inc(p_landed, 16)


def _tiles(w, cols=P):
    k, n = w.shape
    return w.reshape(k // P, P, n // cols, cols).transpose(2, 1, 0, 3)


def _cols(v):
    return v.reshape(-1, P).T


def _weights(i):
    out = np.zeros((N_UNITS, P, UNIT), np.float32)

    def put(name, units):
        units = units.reshape(units.shape[0], P, -1)
        out[BASE[name]:BASE[name] + len(units), :, 0:units.shape[2]] = units

    def paired(w):
        t = _tiles(w).reshape(w.shape[1] // P, P, -1)
        return t.reshape(-1, 2, P, t.shape[2]).transpose(0, 2, 1, 3)

    put("up1", np.stack([_tiles(i["ffn1_w1"][0]), _tiles(i["ffn1_w3"][0])], 2).reshape(FF, P, -1))

    def down(w):
        return _tiles(w).reshape(KC, P, 2, -1).transpose(0, 2, 1, 3).reshape(2 * KC, P, -1)

    put("down1", down(i["ffn1_w2"][0]))
    w_in = i["w_in"][0]
    put("proj", paired(w_in[:, 0:2560]))
    put("kr", _tiles(np.concatenate([np.zeros((D, NOPE), np.float32), w_in[:, 2560:2592]], 1), QK_D))
    uq = _tiles(i["w_uq"][0], QK_D)
    put("uq", uq.reshape(4, 2, P, -1).transpose(0, 2, 1, 3))
    ukv = i["w_ukv"][0].reshape(ML_KV_RANK, NA_HEADS, 2, 64)
    put("ukv_k", _tiles(ukv[:, :, 0].reshape(ML_KV_RANK, 512), 64).transpose(1, 0, 2, 3)[None])
    put("ukv_v", _tiles(ukv[:, :, 1].reshape(ML_KV_RANK, 512), 512))
    gates = _tiles(w_in[:, 2592:])

    def with_branches(g, a, b):
        both = [np.concatenate([g[q * KC:(q + 1) * KC], _tiles(w)], 2) for q, w in ((0, a), (1, b))]
        return np.stack(both, 1).reshape(2 * KC, P, -1)

    put("merge1", with_branches(gates, i["w_o_na"][0], i["w_o_mla"][0]))
    put("out1", paired(i["w_out"][0]))
    put("up2", np.stack([_tiles(i["ffn2_w1"][0]), _tiles(i["ffn2_w3"][0])], 2).reshape(FF, P, -1))
    put("down2", down(i["ffn2_w2"][0]))
    w2 = i["w_in_2"][0]
    put("qk_m", paired(w2[:, 0:1024]))
    put("v_m", _tiles(w2[:, 1024:2048], 256))
    put("o_m", paired(w2[:, 2048:3072]))
    between = np.zeros((D, 28), np.float32)
    put("if_m", _tiles(np.concatenate([w2[:, 3072:3076], between, w2[:, 3076:3080]], 1), 36))
    put("q_sw", paired(w2[:, 3080:4104]))
    put("k_sw", paired(w2[:, 4104:4360]))
    put("v_sw", _tiles(w2[:, 4360:4616], 256))
    put("merge2", with_branches(_tiles(w2[:, 4616:]), i["w_branch_a_2"][0], i["w_branch_b_2"][0]))
    put("out2", paired(i["w_out_2"][0]))
    put("up3", paired(i["w_up_2"][0]))
    put("down3", down(i["w_down_2"][0]))
    put("ple", np.concatenate([_tiles(i["w_ple_gate_2"][0]), _tiles(i["w_ple_proj_2"][0])], 2).reshape(KC, P, -1))
    return out


def _params(i):
    p = np.zeros((P, N_PARAM), np.float32)

    def put(name, a):
        p[0:a.shape[0], PARAM[name]:PARAM[name] + a.shape[1]] = a

    put("b_ada", np.repeat(_cols(i["b_ada"][0]), 2, axis=1))
    put("norm_g", np.repeat(_cols(i["norm_g"][0].reshape(-1)), 2, axis=1))
    put("b_gate", _cols(i["b_gate"][0]))
    put("g_q", _cols(i["g_q_lora"][0]))
    put("g_kv", _cols(i["g_kv_lora"][0]))
    put("mix_g", _cols(i["norm_mix_g_2"][0]))
    put("mlstm_g", _cols(i["mlstm_norm_g_2"][0]))
    put("mlp_g", _cols(i["norm_mlp_g_2"][0]))
    put("ple_g", _cols(i["norm_ple_g_2"][0]))
    put("final_g", _cols(i["final_norm_g_2"]))
    put("conv", i["conv_qk_2"][0].reshape(4, KC, P).transpose(2, 1, 0).reshape(P, -1))
    put("sinks", np.repeat(i["sinks_2"], P, axis=0))
    p[0:4, PARAM["b_if"]] = i["b_if_2"][0, 0:4]
    p[32:36, PARAM["b_if"] + 1] = i["b_if_2"][0, 4:8]
    put("eps", np.full((P, 1), EPS, np.float32))
    return p


def _consts():
    c = np.zeros((P, N_CONST), np.float32)

    def put(name, a):
        c[0:a.shape[0], CONST[name]:CONST[name] + a.shape[1]] = a

    put("ident", np.eye(P))
    put("ones", np.ones((P, P)))
    half = ROPE // 4
    rot = np.zeros((QK_D, QK_D))
    freqs = (10000.0 ** (-np.arange(half, dtype=np.float32) / half)).astype(np.float32)
    tok = np.arange(S)
    cos, sin = np.ones((QK_D, S), np.float32), np.zeros((QK_D, S), np.float32)
    for axis, pos in ((0, tok // GRID_W), (1, tok % GRID_W)):
        at = NOPE + axis * 2 * half
        ang = freqs[:, None] * pos[None, :].astype(np.float32)
        for side in range(2):
            cos[at + side * half:at + (side + 1) * half] = np.cos(ang)
            sin[at + side * half:at + (side + 1) * half] = np.sin(ang)
        for r in range(half):
            rot[at + half + r, at + r] = -1.0
            rot[at + r, at + half + r] = 1.0
    put("rot", rot)
    put("cos", cos)
    put("sin", sin)
    put("select", np.kron(np.eye(4), np.ones((1, P))))
    q, k = np.arange(P)[:, None] % Q_COLS, np.arange(K_COLS)[None, :]
    na = []
    for j in range(N_BLK):
        start = np.clip(j * Q_COLS + q - WIN_W // 2, 0, GRID_W - WIN_W)
        col = K_START[j] + k
        na.append(np.where((col >= start) & (col < start + WIN_W), 0.0, NEG))
    put("na_mask", np.concatenate(na, 1))
    diff = np.arange(P)[:, None] + SW_W - np.arange(2 * P)[None, :]
    put("sw_mask", np.where((diff >= 0) & (diff < SW_W), 0.0, NEG))
    put("causal", np.where(np.arange(P)[None, :] >= np.arange(P)[:, None], 0.0, NEG))
    return c


def _rpb_rows(rpb):
    pad = np.pad(rpb, ((0, 0), (0, 0), (Q_COLS, Q_COLS + 1)))
    out = np.zeros((GRID_H, Q_COLS, NA_HEADS, GRID_H, BIAS_W), np.float32)
    for r in range(GRID_H):
        for c in range(Q_COLS):
            at = WIN_W - 1 - c
            out[r, c] = pad[:, GRID_H - 1 - r:2 * GRID_H - 1 - r, at:at + BIAS_W]
    return out.reshape(P, -1)


def kernel(**inputs):
    import concourse.bacc as _bacc
    from concourse.bass_utils import run_bass_kernel_spmd as _run

    i = {k: np.asarray(v) for k, v in inputs.items()}
    nc = _bacc.Bacc("TRN2", target_bir_lowering=False, num_devices=1)
    tokens = np.concatenate([i["x"][0], i["ctx"][0]], 0)
    arrays = {
        "xT": np.ascontiguousarray(tokens.T.reshape(KC, P, T).transpose(1, 0, 2)),
        "cB": np.ascontiguousarray(np.broadcast_to(np.stack([i["c"][0], i["c_ctx"]]), (P, 2, D))),
        "w_ada": np.ascontiguousarray(i["w_ada"][0].T.reshape(N_MOD * KC, P, D).transpose(1, 0, 2)),
        "params": _params(i),
        "consts": _consts(),
        "weights": _weights(i),
        "rpb": _rpb_rows(i["rpb"][0]),
        "pT": np.ascontiguousarray(i["p_2"][0, 0].T.reshape(2, P, S).transpose(1, 0, 2)),
    }
    aps = {n: nc.dram_tensor(n, a.shape, F32, kind="ExternalInput").ap() for n, a in arrays.items()}
    out = nc.dram_tensor("out", (D, S), F32, kind="ExternalOutput").ap()
    build(nc, aps["xT"], aps["cB"], aps["w_ada"], aps["params"], aps["consts"], aps["weights"], aps["rpb"], aps["pT"], out)
    r = _run(nc, [arrays], core_ids=[0])
    return np.ascontiguousarray(r.results[0]["out"].T)[None]
```
